# Optimizing a Trainium2 kernel written in Bass

```python
import jax, jax.numpy as jnp
from jax import lax
import numpy as np

D_MODEL = 2048
BATCH = 1
SEQ = 128
DEPTH = 1
DEC_BATCH = 1
DEC_SEQ = 256
PAST_LEN = 128

GRID_W = 64
LRU_WIDTH = 1024
LRU_HEADS = 8
LRU_HEAD_DIM = LRU_WIDTH // LRU_HEADS
LRU_CONV = 4
LRU_C = 8.0
CONV_WIDTH = 1024
SHORT_CONV = 3
MIX_WIDTH = LRU_WIDTH + CONV_WIDTH
D_IN = 2 * LRU_WIDTH + 3 * CONV_WIDTH
D_FF = ((8 * D_MODEL // 3 + 255) // 256) * 256
N_MOD = 6
EPS = 1e-6
POS_BASE = 10000.0

kernel_name = "hybrid_rglru_shortconv_diffusion_step"

def rmsnorm(x, g):
    xf = x.astype(jnp.float32)
    y = xf * lax.rsqrt(jnp.mean(xf * xf, axis=-1, keepdims=True) + EPS)
    return (y * g.astype(jnp.float32)).astype(x.dtype)

def modulation(cvec, w_mod, b_mod):
    m = jax.nn.silu(cvec) @ w_mod + b_mod
    return m.reshape(cvec.shape[0], N_MOD, 1, D_MODEL)

def dwconv(x, w, pad):
    return lax.conv_general_dilated(
        x, w[:, None, :].astype(x.dtype), window_strides=(1,), padding=[pad],
        dimension_numbers=("NWC", "WIO", "NWC"), feature_group_count=x.shape[-1])

def block_diag(x, w, b):
    xh = x.reshape(x.shape[0], x.shape[1], LRU_HEADS, LRU_HEAD_DIM)
    y = jnp.einsum("blhd,hde->blhe", xh, w.astype(jnp.float32)) + b.astype(jnp.float32)
    return y.reshape(x.shape)

def rglru_dir(x, w_a, b_a, w_i, b_i, lam, h0, reverse):
    r = jax.nn.sigmoid(block_diag(x, w_a, b_a))
    i = jax.nn.sigmoid(block_diag(x, w_i, b_i))
    log_a = -LRU_C * r * jax.nn.softplus(-lam.astype(jnp.float32))
    a = jnp.exp(log_a)
    u = jnp.sqrt(jnp.maximum(-jnp.expm1(2.0 * log_a), 0.0)) * (i * x)

    def step(h, au):
        a_t, u_t = au
        h = a_t * h + u_t
        return h, h

    h_last, hs = lax.scan(step, h0, (jnp.swapaxes(a, 0, 1), jnp.swapaxes(u, 0, 1)), reverse=reverse)
    return jnp.swapaxes(hs, 0, 1), h_last

def grid_pos_embed(n_tok, dtype):
    rows = n_tok // GRID_W
    r = jnp.repeat(jnp.arange(rows, dtype=jnp.float32), GRID_W)
    col = jnp.tile(jnp.arange(GRID_W, dtype=jnp.float32), rows)
    n_freq = D_MODEL // 4
    freqs = 1.0 / (POS_BASE ** (jnp.arange(n_freq, dtype=jnp.float32) / n_freq))
    er = r[:, None] * freqs
    ec = col[:, None] * freqs
    return jnp.concatenate([jnp.sin(er), jnp.cos(er), jnp.sin(ec), jnp.cos(ec)], axis=-1).astype(dtype)

def trunk_layer(x, mod, h0, g, w_in, cw, cb, w_a, b_a, w_i, b_i, lam, sc_w, w_out, w_gate, w_up, w_down):
    mod = mod.astype(x.dtype)
    hn = rmsnorm(x, g[0]) * (1.0 + mod[:, 1]) + mod[:, 0]
    z = hn @ w_in
    x_lru, y_gate, b_g, c_g, v = jnp.split(
        z, [LRU_WIDTH, 2 * LRU_WIDTH, 2 * LRU_WIDTH + CONV_WIDTH, 2 * LRU_WIDTH + 2 * CONV_WIDTH], axis=-1)
    xc = (dwconv(x_lru, cw, (2, 1)) + cb).astype(jnp.float32)
    h0f = h0.astype(jnp.float32)
    o_f, s_f = rglru_dir(xc, w_a[0], b_a[0], w_i[0], b_i[0], lam[0], h0f[:, 0], False)
    o_b, s_b = rglru_dir(xc, w_a[1], b_a[1], w_i[1], b_i[1], lam[1], h0f[:, 1], True)
    lru_out = (o_f + o_b).astype(x.dtype) * jax.nn.gelu(y_gate)
    sc_out = b_g * dwconv(c_g * v, sc_w, (1, 1))
    m = jnp.concatenate([lru_out, sc_out], axis=-1) @ w_out
    x = x + mod[:, 2] * m
    hn = rmsnorm(x, g[1]) * (1.0 + mod[:, 4]) + mod[:, 3]
    f = (jax.nn.silu(hn @ w_gate) * (hn @ w_up)) @ w_down
    x = x + mod[:, 5] * f
    return x, jnp.stack([s_f, s_b], axis=1)

def setup_inputs(seed: int = 0) -> dict:
    key = jax.random.key(seed)
    ks = jax.random.split(key, 24)
    f32 = jnp.float32
    nrm = lambda k, shape, s: (jax.random.normal(k, shape, f32) * s)
    hd = LRU_HEAD_DIM
    u = jax.random.uniform(ks[14], (DEPTH, 2, LRU_WIDTH), f32, minval=0.9, maxval=0.999)
    a0 = u ** (1.0 / LRU_C)
    lru_lambda = jnp.log(a0) - jnp.log1p(-a0)
    return {
        "x_prompt": nrm(ks[0], (BATCH, SEQ, D_MODEL), 1.0),
        "x_sample": nrm(ks[1], (DEC_BATCH, DEC_SEQ, D_MODEL), 1.0),
        "state_rglru": nrm(ks[2], (DEC_BATCH, DEPTH, 2, LRU_WIDTH), 1.0),
        "c": nrm(ks[3], (DEC_BATCH, D_MODEL), 1.0),
        "c_ctx": nrm(ks[4], (D_MODEL,), 1.0),
        "w_mod": nrm(ks[5], (DEPTH, D_MODEL, N_MOD * D_MODEL), 0.5 * D_MODEL ** -0.5),
        "b_mod": nrm(ks[6], (DEPTH, N_MOD * D_MODEL), 0.02),
        "norm_g": 1.0 + nrm(ks[7], (DEPTH, 2, D_MODEL), 0.01),
        "w_in": nrm(ks[8], (DEPTH, D_MODEL, D_IN), D_MODEL ** -0.5),
        "lru_conv_w": nrm(ks[9], (DEPTH, LRU_CONV, LRU_WIDTH), LRU_CONV ** -0.5),
        "lru_conv_b": nrm(ks[10], (DEPTH, LRU_WIDTH), 0.01),
        "lru_w_a": nrm(ks[11], (DEPTH, 2, LRU_HEADS, hd, hd), hd ** -0.5),
        "lru_b_a": nrm(ks[12], (DEPTH, 2, LRU_HEADS, hd), 0.01),
        "lru_w_i": nrm(ks[13], (DEPTH, 2, LRU_HEADS, hd, hd), hd ** -0.5),
        "lru_b_i": nrm(ks[15], (DEPTH, 2, LRU_HEADS, hd), 0.01),
        "lru_lambda": lru_lambda,
        "sc_conv_w": nrm(ks[16], (DEPTH, SHORT_CONV, CONV_WIDTH), SHORT_CONV ** -0.5),
        "w_out": nrm(ks[17], (DEPTH, MIX_WIDTH, D_MODEL), MIX_WIDTH ** -0.5),
        "w_gate": nrm(ks[18], (DEPTH, D_MODEL, D_FF), D_MODEL ** -0.5),
        "w_up": nrm(ks[19], (DEPTH, D_MODEL, D_FF), D_MODEL ** -0.5),
        "w_down": nrm(ks[20], (DEPTH, D_FF, D_MODEL), D_FF ** -0.5),
        "final_g": 1.0 + nrm(ks[21], (D_MODEL,), 0.01),
    }

def reference(x_prompt, x_sample, state_rglru, c, c_ctx, w_mod, b_mod, norm_g, w_in, lru_conv_w, lru_conv_b,
              lru_w_a, lru_b_a, lru_w_i, lru_b_i, lru_lambda, sc_conv_w, w_out, w_gate, w_up, w_down, final_g):
    xc = x_prompt
    h_zero = jnp.zeros((x_prompt.shape[0], 2, LRU_WIDTH), jnp.float32)
    ctx_states = []
    for l in range(DEPTH):
        mod_ctx = modulation(c_ctx[None, :], w_mod[l], b_mod[l])
        xc, st = trunk_layer(xc, mod_ctx, h_zero, norm_g[l], w_in[l], lru_conv_w[l], lru_conv_b[l],
                             lru_w_a[l], lru_b_a[l], lru_w_i[l], lru_b_i[l], lru_lambda[l], sc_conv_w[l],
                             w_out[l], w_gate[l], w_up[l], w_down[l])
        ctx_states.append(st)
    y_prompt = rmsnorm(xc, final_g)
    new_state = jnp.stack(ctx_states, axis=1).astype(x_prompt.dtype)

    xs = x_sample + grid_pos_embed(x_sample.shape[1], x_sample.dtype)[None]
    for l in range(DEPTH):
        mod_lat = modulation(c, w_mod[l], b_mod[l])
        xs, _ = trunk_layer(xs, mod_lat, state_rglru[:, l], norm_g[l], w_in[l], lru_conv_w[l], lru_conv_b[l],
                            lru_w_a[l], lru_b_a[l], lru_w_i[l], lru_b_i[l], lru_lambda[l], sc_conv_w[l],
                            w_out[l], w_gate[l], w_up[l], w_down[l])
    y_sample = rmsnorm(xs, final_g)
    return (y_prompt, y_sample, new_state)


_drawn_inputs = setup_inputs


def setup_inputs(seed=0):
    import zlib

    import numpy as np

    out = dict(_drawn_inputs(seed))
    spreads = {}
    factors = {'norm_g': 25.83,
     'lru_b_a': 58.089,
     'lru_b_i': 48.353,
     'final_g': 158.322,
     'state_rglru': 64.0,
     'lru_conv_b': 35.264}
    for name, (base, spread) in spreads.items():
        noise = np.random.default_rng([zlib.crc32(name.encode()), seed]).standard_normal(out[name].shape)
        drawn = base * np.exp(spread * noise) if base else spread * noise
        out[name] = __import__('jax').numpy.asarray(drawn.astype(out[name].dtype))
    for name, factor in factors.items():
        out[name] = (out[name] * factor).astype(out[name].dtype)
    return out
```

```python
from contextlib import ExitStack

import concourse.bass as bass
import numpy as np
from concourse import mybir

ALU = mybir.AluOpType
ACT = mybir.ActivationFunctionType
F32 = mybir.dt.float32
F32R = mybir.dt.float32r

P = 128
SLOTS = 4
BLOCK = 1024
BANK = 512
EPS = 1e-6
LRU_C = 8.0
GRID_W = 64
POS_BASE = 10000.0
ATANH_TERMS = [1.0 / n for n in range(17, 1, -2)]


class Tally:

    def __init__(self, sem):
        self.sem, self.base, self.added = sem, 0, 0

    @property
    def value(self):
        return self.base + self.added

    def add(self, instruction):
        instruction.then_inc(self.sem, 1)
        self.added += 1

    def enter(self, i, per_turn):
        self.start, self.per_turn = self.value, per_turn
        self.base, self.added = i * per_turn + self.start, 0

    def leave(self, turns):
        assert self.added == self.per_turn, (self.added, self.per_turn)
        self.base, self.added = self.start + turns * self.per_turn, 0


def build(nc, x_prompt, x_sample, state_rglru, c, c_ctx, w_mod, b_mod, norm_g, w_in, lru_conv_w, lru_conv_b,
          lru_w_a, lru_b_a, lru_w_i, lru_b_i, lru_lambda, sc_conv_w, w_out, w_gate, w_up, w_down, final_g,
          tables, y_prompt, y_sample, new_state):
    D = x_prompt.shape[2]
    CTX = x_prompt.shape[1]
    SMP = x_sample.shape[1]
    T = CTX + SMP
    KT = D // P
    W = lru_lambda.shape[2]
    HEADS = W // P
    FF = w_gate.shape[2]
    GRID_ROWS = SMP // GRID_W
    CHUNK = 4
    CHUNKS = FF // P // CHUNK
    assert CTX == P and SMP == 2 * P and W == 8 * P and D == 2 * W and FF % (CHUNK * P) == 0
    CONV, SC = lru_conv_w.shape[1], sc_conv_w.shape[1]
    SEGMENTS = ((0, 0, CTX), (1, CTX, T))

    PAD = 2
    CTX_AT, SMP_AT = PAD, PAD + CTX + PAD
    PADDED = SMP_AT + SMP + PAD
    RUN = SMP_AT - PAD + SMP

    sizes = [("ctx_c", KT), ("c", KT), ("norm_g", 2 * KT), ("state", 2 * HEADS), ("b_a", 2 * HEADS),
             ("b_i", 2 * HEADS), ("lam", 2 * HEADS),
             ("b_mod", 6 * KT), ("final_g", KT), ("conv_b", HEADS),
             ("conv_w", CONV * HEADS), ("sc_w", SC * HEADS)]
    sources = dict(ctx_c=c_ctx, c=c[0], norm_g=norm_g[0].rearrange("a d -> (a d)"),
                   state=state_rglru[0, 0].rearrange("a d -> (a d)"),
                   b_a=lru_b_a[0].rearrange("a h e -> (a h e)"), b_i=lru_b_i[0].rearrange("a h e -> (a h e)"),
                   lam=lru_lambda[0].rearrange("a d -> (a d)"), b_mod=b_mod[0], final_g=final_g,
                   conv_b=lru_conv_b[0], conv_w=lru_conv_w[0].rearrange("a d -> (a d)"),
                   sc_w=sc_conv_w[0].rearrange("a d -> (a d)"))
    groups = [sizes[:7], sizes[7:10], sizes[10:]]
    at, column = 0, {}
    for name, rows in sizes:
        column[name] = at
        at += rows
    PARAMS = at

    MOD_FIRST = 2 * D // 512
    MOD_STEPS = 6 * D // 512
    IN_STEPS, OUT_STEPS = w_in.shape[2] // 512, D // 512
    assert MOD_STEPS - MOD_FIRST == IN_STEPS + OUT_STEPS + 2
    N_IN = MOD_FIRST * 8
    N_OUT = N_IN + IN_STEPS * 16
    N_G0 = N_OUT + OUT_STEPS * 16
    N_U0 = N_G0 + 16
    N_G1 = N_U0 + 16
    N_LOOP = N_G1 + 8
    PER_CHUNK = 24
    TURNS = CHUNKS - 2
    N_D = N_LOOP + TURNS * PER_CHUNK
    PHASES = [("x", 0), ("c", 2 * W + W), ("v", 2 * W + 2 * W), ("b", 2 * W), ("y", W)]
    FIRST_LRU = 2

    with ExitStack() as ctx:
        def sb(name, shape, dt=F32):
            return ctx.enter_context(nc.sbuf_tensor(name, shape, dt))

        def sem(name):
            return ctx.enter_context(nc.semaphore(name))

        xT = sb("xT", [P, KT, T])
        act_hi = sb("act_hi", [P, KT, T], F32R)
        act_lo = sb("act_lo", [P, KT, T], F32R)
        stage = sb("stage", [P, KT * T])
        raw = [sb(f"raw{s}", [P, 2 * BLOCK]) for s in range(SLOTS)]
        w_hi = [sb(f"w_hi{s}", [P, BLOCK], F32R) for s in range(SLOTS)]
        w_lo = [sb(f"w_lo{s}", [P, BLOCK], F32R) for s in range(SLOTS)]
        h_hi = sb("h_hi", [P, CHUNK, T], F32R)
        h_lo = sb("h_lo", [P, CHUNK, T], F32R)
        scratch = sb("scratch", [P, 8 * T + 4 * PADDED + 2 * T])
        sumsq = sb("sumsq", [P, T])
        rstd = sb("rstd", [P, T])
        gate_w = sb("gate_w", [P, 4, P])
        mod_row = sb("mod_row", [4, BANK])
        prm = sb("prm", [P, PARAMS])
        modT = sb("modT", [P, 6 * KT, 2])
        gain = sb("gain", [P, 2, KT, 2])
        cond = sb("cond", [P, 2, KT])
        cond_w = sb("cond_w", [P, KT, 4], F32R)
        decay = sb("decay", [P, 3, 2 * HEADS])
        stateT = sb("stateT", [P, 2 * HEADS])
        ident = sb("ident", [P, P])
        ones = sb("ones", [P, P])
        eps = sb("eps", [P, 1])
        select = sb("select", [4, 2])

        x_rows = stage[:].rearrange("p (a d) -> p a d", a=3)
        mix = stage[:].rearrange("p (k t) -> p k t", k=KT)
        silu_g = mix[:, 0:CHUNK, :]
        lru = scratch[:, 0:8 * T].rearrange("p (b d t) -> p b d t", b=4, d=2)
        gate_r, gate_i, decay_t, decay_a = (lru[:, b] for b in range(4))
        normed = [lru[:, b] for b in (0, 1)]
        scaled = [lru[:, b] for b in (2, 3)]
        y_tiles = [scratch[:, b * 4 * T:(b + 1) * 4 * T].rearrange("p (k t) -> p k t", k=4) for b in (0, 1)]
        conv_rows = scratch[:, 8 * T:8 * T + 4 * PADDED].rearrange("p (b n) -> p b n", b=4)
        padded, conv_sum = conv_rows[:, 0:2, :], conv_rows[:, 2:4, :]
        squares = scratch[:, 8 * T:10 * T].rearrange("p (a t) -> p a t", a=2)
        gelu_y = scratch[:, 8 * T + 4 * PADDED:].rearrange("p (a t) -> p a t", a=2)
        prm_rows = scratch[:, 0:3 * P].rearrange("p (g n) -> p g n", g=3)
        small = scratch[:, 3 * P:3 * P + 8 * 2 * HEADS].rearrange("p (a n) -> p a n", a=8)
        POS = GRID_ROWS * (KT // 2) + GRID_W * (KT // 2)
        pos = scratch[:, 8 * T + 2 * T:8 * T + 2 * T + POS]
        pos_row = pos[:, 0:GRID_ROWS * (KT // 2)].rearrange("p (k r) -> p k r", r=GRID_ROWS)
        pos_col = pos[:, GRID_ROWS * (KT // 2):POS].rearrange("p (k w) -> p k w", w=GRID_W)

        psum = ctx.enter_context(nc.psum_tensor("psum", [P, 8, BANK], F32))
        R_BANK, I_BANK, MOD_BANK, SMALL_BANK = 4, 5, 6, 7
        UP_BANKS, FIRST_UP_BANKS = (4, 6), (4, 2)
        DOWN_BANKS = (4, 6, 0, 2, 4, 6, 0, 2)
        V_DRAINED, B_DRAINED, Y_DRAINED = HEADS // 2, 2 * (HEADS // 2), 3 * (HEADS // 2)

        def banks(b, n=2):
            return psum[:, b:b + n, 0:T]

        tables_landed = sem("tables_landed")
        params_landed = sem("params_landed")
        x_landed = sem("x_landed")
        gate_w_landed = sem("gate_w_landed")
        landed = [sem(f"landed{s}") for s in range(SLOTS)]
        hi_ready = sem("hi_ready")
        lo_ready = sem("lo_ready")
        block_done = sem("block_done")
        zeroed = sem("zeroed")
        turned = sem("turned")
        prm_ready = sem("prm_ready")
        silu_ready = sem("silu_ready")
        exp_lam_ready = sem("exp_lam_ready")
        abs_ready = sem("abs_ready")
        cond_hi_ready = sem("cond_hi_ready")
        cond_ready = sem("cond_ready")
        decay_ready = sem("decay_ready")
        x_turned = sem("x_turned")
        ctx_copied = sem("ctx_copied")
        x_ready = sem("x_ready")
        squared = sem("squared")
        summed = sem("summed")
        sum_done = sem("sum_done")
        root_ready = sem("root_ready")
        normed_ready = sem("normed_ready")
        scaled_ready = sem("scaled_ready")
        act_hi_ready = sem("act_hi_ready")
        act_ready = sem("act_ready")
        row_ready = sem("row_ready")
        row_turned = sem("row_turned")
        mod_ready = sem("mod_ready")
        drained = sem("drained")
        padded_ready = sem("padded_ready")
        xc_ready = sem("xc_ready")
        gates_done = sem("gates_done")
        gates_read = sem("gates_read")
        decays_ready = sem("decays_ready")
        power_ready = sem("power_ready")
        root_u_ready = sem("root_u_ready")
        head_done = sem("head_done")
        gelu_ready = sem("gelu_ready")
        x1_ready = sem("x1_ready")
        silu_done = sem("silu_done")
        h_full = sem("h_full")
        h_hi_ready = sem("h_hi_ready")
        h_ready = sem("h_ready")
        down_drained = sem("down_drained")
        y_ready = sem("y_ready")
        y_turned = sem("y_turned")
        y_copied = sem("y_copied")
        state_turned = sem("state_turned")
        state_copied = sem("state_copied")
        dve_step = sem("dve_step")
        stored = sem("stored")

        w_mod_v = w_mod[0].rearrange("(k p) n -> p k n", p=P)
        w_in_v = w_in[0].rearrange("(k p) n -> p k n", p=P)
        w_out_v = w_out[0].rearrange("(k p) n -> p k n", p=P)
        w_gate_v = w_gate[0].rearrange("(k p) n -> p k n", p=P)
        w_up_v = w_up[0].rearrange("(k p) n -> p k n", p=P)
        w_down_v = w_down[0].rearrange("(k p) n -> p k n", p=P)

        def slot_of(block):
            return block % SLOTS

        def raw_of(kind, block):
            if kind == "GM":
                quad, at = divmod(block, 4)
                half, second = at % 2, at // 2
                wide = half == 1
            else:
                quad, at = divmod(block, 4)
                half, second = divmod(at, 2)
                wide = kind != "G"
            slot = 2 * (quad % 2) + half
            if not wide:
                return slot, raw[slot][:].rearrange("p (k n) -> p k n", n=256)[:, 4 * second:4 * second + 4, :]
            view = raw[slot][:].rearrange("p (k n) -> p k n", n=512)
            if kind == "D":
                return slot, view[:, :, 256 * second:256 * second + 256]
            return slot, view[:, 2 * second:2 * second + 2, :]

        def split_view(tile, kind, block):
            n = 512 if kind == "M" or (kind == "GM" and block % 2) else 256
            return tile[slot_of(block)][:].rearrange("p (k n) -> p k n", n=n)

        def landed_by(n, block):
            return (n - block) * 2 + 16 * (block // 8) + 16

        block_ctx = ctx.enter_context(nc.Block())

        @block_ctx.sync
        def _(sp):
            def quad(n, quad_at, halves):
                first = 2 * (quad_at % 2)
                for half, source in enumerate(halves):
                    if not isinstance(n, int) or n >= 8:
                        sp.wait_ge(lo_ready, n - 4)
                    width = source.shape[2]
                    sp.dma_start(raw[first + half][:].rearrange("p (k n) -> p k n", n=width), source)\
                        .then_inc(landed[first + half], 16)

            def held(value):
                return value if isinstance(value, int) else sp.snap(value)

            def mod_half(at, quarter):
                return w_mod_v[:, 4 * quarter:4 * quarter + 4, bass.ds(at, 512)]

            def g_half(view, col, quad_at, k_order=(0, 1)):
                k = 8 * k_order[quad_at % 2]
                return view[:, k:k + 8, bass.ds(col + 256 * (quad_at // 2), 256)]

            def gm_step(n, view, col, m, k_order=(0, 1)):
                at = held(m * 512)
                for q in range(4):
                    quad(n + 4 * q, q, [g_half(view, col, q, k_order), mod_half(at, q)])

            def g_step(n, view, col):
                col = held(col)
                for q in range(2):
                    quad(n + 4 * q, q, [g_half(view, col, 2 * q), g_half(view, col, 2 * q + 1)])

            def d_step(n, chunk):
                first_k = held(chunk * CHUNK)
                for q in range(2):
                    quad(n + 4 * q, q, [w_down_v[:, bass.ds(first_k, CHUNK), 1024 * q + 512 * h:1024 * q + 512 * h + 512]
                                        for h in range(2)])

            def m_step(n, m):
                at = held(m * 512)
                for q in range(2):
                    quad(n + 4 * q, q, [mod_half(at, 2 * q), mod_half(at, 2 * q + 1)])

            sp.dma_start(x_rows[:, 0, :], x_prompt[0]).then_inc(x_landed, 16)
            for a in range(2):
                sp.dma_start(x_rows[:, 1 + a, :], x_sample[0, a * P:(a + 1) * P, :]).then_inc(x_landed, 16)
            m_step(0, 0)
            with sp.Fori(1, MOD_FIRST) as i:
                m_step(i * 8, i)
            for phase, (_, col) in enumerate(PHASES):
                with sp.Fori(0, 2) as i:
                    gm_step(i * 16 + N_IN + 32 * phase, w_in_v, i * 512 + col, i + (MOD_FIRST + 2 * phase))
            with sp.Fori(1, OUT_STEPS + 1) as i:
                gm_step(i * 16 + (N_OUT - 16), w_out_v, i * 512 - 512, i + (MOD_FIRST + IN_STEPS - 1), k_order=(1, 0))
            gm_step(N_G0, w_gate_v, 0, MOD_STEPS - 2)
            gm_step(N_U0, w_up_v, 0, MOD_STEPS - 1)
            g_step(N_G1, w_gate_v, 512)
            with sp.Fori(0, TURNS) as i:
                n = i * PER_CHUNK + N_LOOP
                d_step(n, i)
                g_step(n + 8, w_up_v, i * 512 + 512)
                g_step(n + 16, w_gate_v, i * 512 + 1024)
            d_step(N_D, CHUNKS - 2)
            g_step(N_D + 8, w_up_v, (CHUNKS - 1) * 512)
            d_step(N_D + 16, CHUNKS - 1)
            for g in range(4):
                sp.wait_ge(y_copied, g + 1)
                cols = slice(512 * g, 512 * g + 512)
                sp.dma_start(y_prompt[0, :, cols], x_rows[:, 0, cols]).then_inc(stored, 16)
                for a in range(2):
                    sp.dma_start(y_sample[0, a * P:(a + 1) * P, cols], x_rows[:, 1 + a, cols]).then_inc(stored, 16)
            sp.wait_ge(state_copied, 1)
            sp.dma_start(new_state[0, 0].rearrange("a (h e) -> (a h) e", e=P), sumsq[0:2 * HEADS, 0:P])\
                .then_inc(stored, 16)
            sp.wait_ge(stored, 16 * 13)

        @block_ctx.gpsimd
        def _(pool):
            pool.dma_start(ident[:], tables[:, POS:POS + P]).then_inc(tables_landed, 16)
            for g, group in enumerate(groups):
                row = 0
                for name, rows in group:
                    pool.dma_start(prm_rows[row:row + rows, g, :], sources[name].rearrange("(r e) -> r e", e=P))\
                        .then_inc(params_landed, 16)
                    row += rows
            pool.dma_start(pos, tables[:, 0:POS]).then_inc(tables_landed, 16)
            pool.dma_start(select[:], tables[0:4, POS + P:POS + P + 2]).then_inc(tables_landed, 16)
            pool.memset(ones[:], 1.0).then_inc(zeroed, 1)
            pool.memset(eps[:], EPS).then_inc(zeroed, 1)
            pool.wait_ge(summed, KT)
            pool.memset(padded, 0.0).then_inc(zeroed, 1)
            for h in range(HEADS):
                if h:
                    pool.wait_ge(gates_done, 2 * h)
                pool.dma_start(gate_w[:, 0:2, :], lru_w_a[0, :, h].rearrange("a d e -> d a e"))\
                    .then_inc(gate_w_landed, 16)
                pool.dma_start(gate_w[:, 2:4, :], lru_w_i[0, :, h].rearrange("a d e -> d a e"))\
                    .then_inc(gate_w_landed, 16)

        @block_ctx.scalar
        def _(act):
            def round_blocks(kind, n, blocks):
                for b in blocks:
                    slot, source = raw_of(kind, b)
                    act.wait_ge(landed[slot], landed_by(n + b, b))
                    if not isinstance(n, int) or n + b >= SLOTS:
                        act.wait_ge(block_done, n + b - (SLOTS - 1))
                    act.activation(split_view(w_hi, kind, b), source, ACT.Copy).then_inc(hi_ready, 1)

            def root_of_mean_square(which):
                act.wait_ge(sum_done, which + 1)
                act.activation(rstd[:], psum[:, SMALL_BANK, 0:T], ACT.Sqrt, bias=eps[:], scale=1.0 / D)\
                    .then_inc(root_ready, 1)

            def norm_tiles(which, shift):
                with act.Fori(0, KT // 4) as i:
                    for b in range(2):
                        pair = i * 2 + b
                        done = pair + which * (KT // 2)
                        act.wait_ge(normed_ready, done + 1)
                        for a in range(2):
                            k = i * 4 + (2 * b + a)
                            act.activation(scaled[b][:, a, CTX:T], normed[b][:, a, CTX:T], ACT.Identity,
                                           bias=modT[:, bass.ds(k + shift * KT, 1), 1],
                                           scale=gain[:, which, bass.ds(k, 1), 1]).then_inc(scaled_ready, 1)
                        act.wait_ge(scaled_ready, done * 2 + 2)
                        act.activation(act_hi[:, bass.ds(pair * 2, 2), :], scaled[b], ACT.Copy)\
                            .then_inc(act_hi_ready, 1)

            act.wait_ge(prm_ready, 1)
            act.activation(cond[:], prm[:, 0:2 * KT].rearrange("p (a k) -> p a k", a=2), ACT.Silu)\
                .then_inc(silu_ready, 1)
            act.wait_ge(silu_ready, 1)
            act.activation(cond_w[:].rearrange("p k a -> p a k")[:, 0:2, :], cond[:], ACT.Copy)\
                .then_inc(cond_hi_ready, 1)
            lam = prm[:, column["lam"]:column["lam"] + 2 * HEADS]
            act.activation(small[:, 0, :], lam, ACT.Abs).then_inc(abs_ready, 1)
            act.wait_ge(abs_ready, 1)
            act.activation(small[:, 1, :], small[:, 0, :], ACT.Exp, scale=-1.0).then_inc(exp_lam_ready, 1)
            for k in range(KT):
                act.wait_ge(x_turned, k + 1)
                act.activation(xT[:, k, 0:CTX], psum[:, k % 4, 0:CTX], ACT.Copy).then_inc(ctx_copied, 1)
                if k >= 1:
                    act.wait_ge(x_ready, k)
                    if k >= 3:
                        act.wait_ge(summed, k - 2)
                    act.activation(squares[:, (k - 1) % 2, :], xT[:, k - 1, :], ACT.Square).then_inc(squared, 1)
            act.wait_ge(x_ready, KT)
            act.wait_ge(summed, KT - 2)
            act.activation(squares[:, (KT - 1) % 2, :], xT[:, KT - 1, :], ACT.Square).then_inc(squared, 1)
            root_of_mean_square(0)
            round_blocks("M", 0, range(8))
            with act.Fori(1, MOD_FIRST) as i:
                round_blocks("M", i * 8, range(8))

            for step in range(IN_STEPS):
                n = N_IN + 16 * step
                phase = PHASES[step // 2][0]
                before = PHASES[(step - 1) // 2][0] if step else None
                head = step - FIRST_LRU

                def pad_rows(pair, bank, n_done):
                    act.wait_ge(block_done, n_done)
                    for a in range(2):
                        tile = 2 * pair + a
                        if tile >= 2:
                            act.wait_ge(xc_ready, tile - 1)
                        else:
                            act.wait_ge(zeroed, 3)
                        act.activation(padded[:, a, CTX_AT:CTX_AT + CTX], psum[:, bank + a, 0:CTX], ACT.Copy)
                        act.activation(padded[:, a, SMP_AT:SMP_AT + SMP], psum[:, bank + a, CTX:T], ACT.Copy)\
                            .then_inc(padded_ready, 1)

                def gelu(pair, bank, n_done):
                    act.wait_ge(block_done, n_done)
                    if pair:
                        act.wait_ge(drained, Y_DRAINED + pair)
                    act.activation(gelu_y, banks(bank), ACT.Gelu_apprx_tanh).then_inc(gelu_ready, 1)

                round_blocks("GM", n, range(0, 4))
                if step == 0:
                    norm_tiles(0, 0)
                if before == "x":
                    pad_rows(2 * step - 1, 2, n - 1)
                if before == "y":
                    gelu(2 * (step - 8) - 1, 2, n - 1)
                round_blocks("GM", n, range(4, 5))
                if head >= 0:
                    act.wait_ge(gates_done, 2 * head + 1)
                    if head:
                        act.wait_ge(head_done, head)
                    for bank, bias, to in ((R_BANK, "b_a", gate_r), (I_BANK, "b_i", gate_i)):
                        at_bias = column[bias] + head
                        last = act.activation(to[:, 0, :], psum[:, bank, 0:T], ACT.Sigmoid,
                                              bias=prm[:, at_bias:at_bias + 1])
                    last.then_inc(gates_read, 1)
                round_blocks("GM", n, range(5, 12))
                if phase == "x":
                    pad_rows(2 * step, 0, n + 7)
                if phase == "y":
                    gelu(2 * (step - 8), 0, n + 7)
                round_blocks("GM", n, range(12, 13))
                if head >= 0:
                    act.wait_ge(gates_done, 2 * head + 2)
                    for bank, bias, to in ((R_BANK, "b_a", gate_r), (I_BANK, "b_i", gate_i)):
                        at_bias = column[bias] + HEADS + head
                        last = act.activation(to[:, 1, :], psum[:, bank, 0:T], ACT.Sigmoid,
                                              bias=prm[:, at_bias:at_bias + 1])
                    last.then_inc(gates_read, 1)
                    act.wait_ge(gates_read, 2 * head + 2)
                    if head == 0:
                        act.wait_ge(decay_ready, 3)
                    for d in range(2):
                        lam_at = d * HEADS + head
                        act.activation(decay_t[:, d, :], gate_r[:, d, :], ACT.Tanh,
                                       scale=decay[:, 0, lam_at:lam_at + 1])
                    for d in range(2):
                        lam_at = d * HEADS + head
                        act.activation(decay_a[:, d, :], gate_r[:, d, :], ACT.Exp,
                                       scale=decay[:, 1, lam_at:lam_at + 1])
                        last = act.activation(gate_r[:, d, :], gate_r[:, d, :], ACT.Exp,
                                              scale=decay[:, 2, lam_at:lam_at + 1])
                    last.then_inc(decays_ready, 1)
                round_blocks("GM", n, range(13, 16))
                if head >= 0:
                    act.wait_ge(power_ready, head + 1)
                    act.activation(decay_t, decay_t, ACT.Sqrt).then_inc(root_u_ready, 1)

            def square_pair(pair, pairs_before=KT):
                act.wait_ge(x1_ready, pair + 1)
                act.wait_ge(summed, pair + pairs_before)
                act.activation(squares, xT[:, bass.ds(pair * 2, 2), :], ACT.Square).then_inc(squared, 1)

            def out_step(n, i, first):
                round_blocks("GM", n, range(0, 4))
                if first:
                    act.wait_ge(block_done, n - 1)
                    act.wait_ge(drained, Y_DRAINED + 3)
                    act.activation(gelu_y, banks(2), ACT.Gelu_apprx_tanh).then_inc(gelu_ready, 1)
                    for j in range(KT // 2):
                        pair = (j + KT // 4) % (KT // 2)
                        if pair < KT // 4:
                            act.wait_ge(drained, Y_DRAINED + pair + 1)
                        else:
                            act.wait_ge(drained, B_DRAINED + pair - KT // 4 + 1)
                        act.activation(act_hi[:, 2 * pair:2 * pair + 2, :], mix[:, 2 * pair:2 * pair + 2, :],
                                       ACT.Copy).then_inc(act_hi_ready, 1)
                else:
                    square_pair(i * 2 - 1)
                round_blocks("GM", n, range(4, 12))
                square_pair(i * 2)
                round_blocks("GM", n, range(12, 16))

            out_step(N_OUT, 0, True)
            with act.Fori(1, OUT_STEPS) as i:
                out_step(i * 16 + N_OUT, i, False)

            def silu_pair(chunk, pair, n_done):
                act.wait_ge(block_done, n_done)
                if not isinstance(chunk, int) or chunk:
                    act.wait_ge(h_ready, chunk * 2 + (pair - 1))
                act.activation(silu_g[:, 2 * pair:2 * pair + 2, :], banks(2 * pair), ACT.Silu).then_inc(silu_done, 1)

            def round_h(chunk, pair, n_done):
                act.wait_ge(block_done, n_done)
                act.wait_ge(h_full, chunk * 2 + (pair + 1))
                act.activation(h_hi[:, 2 * pair:2 * pair + 2, :], silu_g[:, 2 * pair:2 * pair + 2, :], ACT.Copy)\
                    .then_inc(h_hi_ready, 1)

            round_blocks("GM", N_G0, range(0, 4))
            square_pair(KT // 2 - 1)
            root_of_mean_square(1)
            norm_tiles(1, 3)
            round_blocks("GM", N_G0, range(4, 12))
            silu_pair(0, 0, N_G0 + 7)
            round_blocks("GM", N_G0, range(12, 16))
            round_blocks("GM", N_U0, range(0, 4))
            silu_pair(0, 1, N_G0 + 15)
            round_blocks("GM", N_U0, range(4, 13))
            round_h(0, 0, N_U0)
            round_blocks("GM", N_U0, range(13, 16))

            def gate_step(n, chunk):
                round_blocks("G", n, range(0, 4))
                round_h(chunk - 1, 1, n - 1)
                round_blocks("G", n, range(4, 8))
                silu_pair(chunk, 0, n + 4)

            def down_step(n, chunk):
                round_blocks("D", n, range(0, 4))
                silu_pair(chunk + 1, 1, n)
                round_blocks("D", n, range(4, 8))

            def up_step(n, chunk):
                round_blocks("G", n, range(0, 8))
                round_h(chunk, 0, n)

            gate_step(N_G1, 1)
            with act.Fori(0, TURNS) as i:
                n = i * PER_CHUNK + N_LOOP
                down_step(n, i)
                up_step(n + 8, i + 1)
                gate_step(n + 16, i + 2)
            down_step(N_D, CHUNKS - 2)
            up_step(N_D + 8, CHUNKS - 1)
            round_blocks("D", N_D + 16, range(0, 4))
            round_h(CHUNKS - 1, 1, N_D + 16)
            round_blocks("D", N_D + 16, range(4, 8))
            for pair in range(KT // 2):
                act.wait_ge(down_drained, 8 * (CHUNKS - 1) + pair + 1)
                act.wait_ge(summed, KT + KT // 2 + pair)
                act.activation(squares, xT[:, 2 * pair:2 * pair + 2, :], ACT.Square).then_inc(squared, 1)
            root_of_mean_square(2)
            for g in range(4):
                act.wait_ge(y_turned, g + 1)
                act.activation(x_rows[:, :, 512 * g:512 * g + 512], psum[:, 3 * (g % 2):3 * (g % 2) + 3, :],
                               ACT.Copy).then_inc(y_copied, 1)
            act.wait_ge(state_turned, 1)
            act.wait_ge(y_ready, 4)
            act.activation(sumsq[0:2 * HEADS, 0:P], psum[0:2 * HEADS, SMALL_BANK, 0:P], ACT.Copy)\
                .then_inc(state_copied, 1)

        @block_ctx.vector
        def _(dve):
            own = Tally(dve_step)

            def then(instruction):
                own.add(instruction)
                dve.wait_ge(own.sem, own.value)

            def subtract_blocks(kind, n, blocks):
                for b in blocks:
                    _, source = raw_of(kind, b)
                    dve.wait_ge(hi_ready, n + b + 1)
                    dve.tensor_tensor(split_view(w_lo, kind, b), source, split_view(w_hi, kind, b).bitcast(F32),
                                      ALU.subtract).then_inc(lo_ready, 1)

            def copy_row(m, n_done):
                dve.wait_ge(block_done, n_done)
                dve.tensor_copy(mod_row[:], psum[0:4, MOD_BANK, :]).then_inc(row_ready, 1)

            def add_bias(m):
                dve.wait_ge(row_turned, m + 1)
                at = column["b_mod"]
                dve.tensor_tensor(modT[:, bass.ds(m * 4, 4), :],
                                  psum[:, SMALL_BANK, 0:8].rearrange("p (k a) -> p k a", a=2),
                                  prm[:, bass.ds(m * 4 + at, 4)].rearrange("p (k a) -> p k a", a=1)
                                  .broadcast_to([P, 4, 2]), ALU.add).then_inc(mod_ready, 1)

            def make_gain(which, scale):
                at = column["norm_g"] + which * KT
                for a in range(2):
                    last = dve.scalar_tensor_tensor(gain[:, which, :, a], modT[:, scale * KT:(scale + 1) * KT, a],
                                                    1.0, prm[:, at:at + KT], ALU.add, ALU.mult)
                then(last)

            def make_rstd(which):
                dve.wait_ge(root_ready, which + 1)
                then(dve.reciprocal(rstd[:], rstd[:]))

            def norm_tiles(which, shift):
                pairs = KT // 2
                rstd2 = rstd[:].rearrange("p (a t) -> p a t", a=1).broadcast_to([P, 2, T])

                def scale_pair(pair, b):
                    then(dve.tensor_tensor(normed[b], xT[:, bass.ds(pair * 2, 2), :], rstd2, ALU.mult))
                    for a in range(2):
                        k = pair * 2 + a
                        last = dve.tensor_scalar(scaled[b][:, a, 0:CTX], normed[b][:, a, 0:CTX],
                                                 gain[:, which, bass.ds(k, 1), 0],
                                                 modT[:, bass.ds(k + shift * KT, 1), 0], ALU.mult, ALU.add)
                    last.then_inc(normed_ready, 1)

                def low_pair(pair, b):
                    dve.wait_ge(act_hi_ready, pair + 1 + which * 2 * pairs)
                    dve.tensor_tensor(act_lo[:, bass.ds(pair * 2, 2), :], scaled[b],
                                      act_hi[:, bass.ds(pair * 2, 2), :].bitcast(F32),
                                      ALU.subtract).then_inc(act_ready, 1)

                scale_pair(0, 0)
                scale_pair(1, 1)
                with dve.Fori(0, pairs // 2 - 1) as i:
                    own.enter(i, 2)
                    for b in range(2):
                        low_pair(i * 2 + b, b)
                        scale_pair(i * 2 + (b + 2), b)
                    own.leave(pairs // 2 - 1)
                low_pair(pairs - 2, 0)
                low_pair(pairs - 1, 1)

            def add_squares(first, parts):
                dve.wait_ge(squared, first)
                for part in parts[:-1]:
                    then(dve.tensor_tensor(sumsq[:], sumsq[:], part, ALU.add))
                own_last = dve.tensor_tensor(sumsq[:], sumsq[:], parts[-1], ALU.add)
                own_last.then_inc(summed, 1)

            dve.wait_ge(turned, len(groups))
            row = 0
            for g, group in enumerate(groups):
                rows = sum(r for _, r in group)
                dve.tensor_copy(prm[:, row:row + rows], psum[:, SMALL_BANK, g * P:g * P + rows])\
                    .then_inc(prm_ready, 1)
                row += rows
            dve.wait_ge(cond_hi_ready, 1)
            parts = cond_w[:].rearrange("p k a -> p a k")
            dve.tensor_tensor(parts[:, 2:4, :], cond[:], parts[:, 0:2, :].bitcast(F32), ALU.subtract)\
                .then_inc(cond_ready, 1)
            dve.wait_ge(exp_lam_ready, 1)
            dve.wait_ge(prm_ready, 3)
            lam = prm[:, column["lam"]:column["lam"] + 2 * HEADS]
            e, s, q, series, softplus = (small[:, j, :] for j in range(1, 6))
            then(dve.tensor_scalar(s, e, 2.0, None, ALU.add))
            then(dve.reciprocal(s, s))
            then(dve.tensor_tensor(s, s, e, ALU.mult))
            then(dve.tensor_tensor(q, s, s, ALU.mult))
            then(dve.tensor_scalar(series, q, ATANH_TERMS[0], None, ALU.mult))
            for term in ATANH_TERMS[1:]:
                then(dve.scalar_tensor_tensor(series, series, term, q, ALU.add, ALU.mult))
            then(dve.scalar_tensor_tensor(series, series, 1.0, s, ALU.add, ALU.mult))
            then(dve.tensor_scalar(softplus, lam, -1.0, 0.0, ALU.mult, ALU.max))
            then(dve.scalar_tensor_tensor(softplus, series, 2.0, softplus, ALU.mult, ALU.add))
            for j, factor in enumerate((LRU_C, -LRU_C, -2.0 * LRU_C)):
                dve.tensor_scalar(decay[:, j, :], softplus, factor, None, ALU.mult).then_inc(decay_ready, 1)

            then(dve.memset(sumsq[:], 0.0))
            dve.wait_ge(tables_landed, 48)
            for k in range(KT):
                dve.wait_ge(x_turned, k + 1)
                dve.wait_ge(ctx_copied, k + 1)
                if k < KT // 2:
                    embed = pos_row[:, k, :].rearrange("p (r w) -> p r w", w=1).broadcast_to([P, GRID_ROWS, GRID_W])
                else:
                    embed = pos_col[:, k - KT // 2, :].rearrange("p (r w) -> p r w", r=1)\
                        .broadcast_to([P, GRID_ROWS, GRID_W])
                dve.tensor_tensor(xT[:, k, CTX:T].rearrange("p (r w) -> p r w", w=GRID_W),
                                  psum[:, k % 4, CTX:T].rearrange("p (r w) -> p r w", w=GRID_W), embed, ALU.add)\
                    .then_inc(x_ready, 1)
                if k >= 1:
                    if k >= 2:
                        dve.wait_ge(summed, k - 1)
                    add_squares(k, [squares[:, (k - 1) % 2, :]])
            dve.wait_ge(summed, KT - 1)
            add_squares(KT, [squares[:, (KT - 1) % 2, :]])

            dve.wait_ge(x_ready, KT)
            dve.wait_ge(zeroed, 3)
            subtract_blocks("M", 0, range(8))
            with dve.Fori(1, MOD_FIRST) as i:
                n = i * 8
                subtract_blocks("M", n, range(0, 4))
                copy_row(i - 1, n)
                subtract_blocks("M", n, range(4, 8))
                add_bias(i - 1)

            def convolve(tile, row, weights, taps, first, to, scalar_bias):
                w = [prm[:, column[weights] + k * HEADS + tile:column[weights] + k * HEADS + tile + 1]
                     for k in range(taps)]
                source = padded[:, row, :]
                total = conv_sum[:, row, 0:RUN]
                if scalar_bias is None:
                    then(dve.tensor_scalar(total, source[:, first:first + RUN], w[0], None, ALU.mult))
                else:
                    then(dve.tensor_scalar(total, source[:, first:first + RUN], w[0], scalar_bias,
                                           ALU.mult, ALU.add))
                for k in range(1, taps - 1):
                    then(dve.scalar_tensor_tensor(total, source[:, first + k:first + k + RUN], w[k], total,
                                                  ALU.mult, ALU.add))
                k = taps - 1
                for start, at, length in ((0, 0, CTX), (CTX, SMP_AT - PAD, SMP)):
                    last = dve.scalar_tensor_tensor(to[:, start:start + length],
                                                    source[:, first + k + at:first + k + at + length], w[k],
                                                    total[:, at:at + length], ALU.mult, ALU.add)
                return last

            def drain_pair(phase, pair, bank, n_done):
                dve.wait_ge(block_done, n_done)
                own_before = {"v": pair + 1, "b": V_DRAINED + pair + 1}.get(phase)
                if own_before:
                    dve.wait_ge(drained, own_before)
                tiles = slice(2 * pair, 2 * pair + 2)
                gates = slice(HEADS + 2 * pair, HEADS + 2 * pair + 2)
                if phase == "x":
                    for a in range(2):
                        tile = 2 * pair + a
                        dve.wait_ge(padded_ready, tile + 1)
                        bias = column["conv_b"] + tile
                        convolve(tile, a, "conv_w", CONV, 0, mix[:, tile, :], prm[:, bias:bias + 1])\
                            .then_inc(xc_ready, 1)
                elif phase == "c":
                    dve.tensor_copy(mix[:, gates, :], banks(bank)).then_inc(drained, 1)
                elif phase == "v":
                    for a in range(2):
                        tile = 2 * pair + a
                        gated = mix[:, HEADS + tile, :]
                        dve.tensor_tensor(padded[:, a, CTX_AT:CTX_AT + CTX], psum[:, bank + a, 0:CTX],
                                          gated[:, 0:CTX], ALU.mult)
                        then(dve.tensor_tensor(padded[:, a, SMP_AT:SMP_AT + SMP], psum[:, bank + a, CTX:T],
                                               gated[:, CTX:T], ALU.mult))
                        last = convolve(tile, a, "sc_w", SC, 1, gated, None)
                        if a == 0:
                            then(last)
                    last.then_inc(drained, 1)
                elif phase == "b":
                    dve.tensor_tensor(mix[:, gates, :], mix[:, gates, :], banks(bank), ALU.mult)\
                        .then_inc(drained, 1)
                else:
                    dve.wait_ge(gelu_ready, pair + 1)
                    dve.wait_ge(head_done, 2 * pair + 2)
                    dve.tensor_tensor(mix[:, tiles, :], mix[:, tiles, :], gelu_y, ALU.mult).then_inc(drained, 1)

            def powers(head):
                dve.wait_ge(decays_ready, head + 1)
                dve.wait_ge(xc_ready, head + 1)
                both = mix[:, head:head + 1, :].broadcast_to([P, 2, T])
                then(dve.tensor_scalar(gate_r, gate_r, 1.0, None, ALU.add))
                dve.scalar_tensor_tensor(decay_t, decay_t, 0.0, gate_r, ALU.max, ALU.mult).then_inc(power_ready, 1)
                then(dve.tensor_tensor(gate_i, gate_i, both, ALU.mult))

            def scans(head):
                dve.wait_ge(root_u_ready, head + 1)
                then(dve.tensor_tensor(gate_i, gate_i, decay_t, ALU.mult))
                for d in range(2):
                    a, u, h = decay_a[:, d, :], gate_i[:, d, :], gate_r[:, d, :]
                    s = column["state"] + d * HEADS + head
                    for start, end, initial in ((0, CTX, 0.0), (CTX, T, prm[:, s:s + 1])):
                        tokens = slice(start, end) if d == 0 else slice(end - 1, start - 1 if start else None, -1)
                        last = dve.tensor_tensor_scan(h[:, tokens], a[:, tokens], u[:, tokens], initial,
                                                      ALU.mult, ALU.add)
                then(last)
                for d, token in ((0, CTX - 1), (1, 0)):
                    s = d * HEADS + head
                    dve.tensor_copy(stateT[:, s:s + 1], gate_r[:, d, token:token + 1])
                dve.tensor_tensor(mix[:, head, :], gate_r[:, 0, :], gate_r[:, 1, :], ALU.add)\
                    .then_inc(head_done, 1)

            for step in range(IN_STEPS):
                n = N_IN + 16 * step
                phase, turn = PHASES[step // 2][0], step % 2
                before = PHASES[(step - 1) // 2][0]
                head = step - FIRST_LRU
                subtract_blocks("GM", n, range(0, 2))
                if head >= 1:
                    scans(head - 1)
                subtract_blocks("GM", n, range(2, 4))
                copy_row(MOD_FIRST + step - 1, n)
                if step == 0:
                    add_bias(MOD_FIRST - 1)
                    dve.wait_ge(mod_ready, MOD_FIRST)
                    make_gain(0, 1)
                    make_rstd(0)
                    norm_tiles(0, 0)
                else:
                    drain_pair(before, 2 * ((step - 1) % 2) + 1, 2, n - 1)
                subtract_blocks("GM", n, range(4, 12))
                if step:
                    add_bias(MOD_FIRST + step - 1)
                drain_pair(phase, 2 * turn, 0, n + 7)
                subtract_blocks("GM", n, range(12, 15))
                if head >= 0:
                    powers(head)
                subtract_blocks("GM", n, range(15, 16))

            def residual_pair(pair, bank, n_done):
                dve.wait_ge(block_done, n_done)
                for a in range(2):
                    k = pair * 2 + a
                    for seg, start, end in SEGMENTS:
                        last = dve.scalar_tensor_tensor(
                            xT[:, bass.ds(k, 1), start:end].rearrange("p a t -> p (a t)"),
                            psum[:, bank + a, start:end],
                            modT[:, bass.ds(k + 2 * KT, 1), seg],
                            xT[:, bass.ds(k, 1), start:end].rearrange("p a t -> p (a t)"), ALU.mult, ALU.add)
                    if a == 1:
                        last.then_inc(x1_ready, 1)
            def add_pair(pair):
                dve.wait_ge(squared, pair + (KT + 1))
                then(dve.tensor_tensor(sumsq[:], sumsq[:], squares[:, 0, :], ALU.add))
                dve.tensor_tensor(sumsq[:], sumsq[:], squares[:, 1, :], ALU.add).then_inc(summed, 1)
                dve.wait_ge(summed, pair + (KT + 1))

            def out_step(n, i, first):
                subtract_blocks("GM", n, range(0, 2))
                if first:
                    scans(HEADS - 1)
                subtract_blocks("GM", n, range(2, 4))
                copy_row(None, n)
                if first:
                    drain_pair("y", 3, 2, n - 1)
                    dve.wait_ge(mod_ready, 3 * KT // 4)
                    then(dve.memset(sumsq[:], 0.0))
                    for j in range(KT // 2):
                        pair = (j + KT // 4) % (KT // 2)
                        dve.wait_ge(act_hi_ready, KT // 2 + j + 1)
                        dve.tensor_tensor(act_lo[:, 2 * pair:2 * pair + 2, :], mix[:, 2 * pair:2 * pair + 2, :],
                                          act_hi[:, 2 * pair:2 * pair + 2, :].bitcast(F32), ALU.subtract)\
                            .then_inc(act_ready, 1)
                else:
                    residual_pair(i * 2 - 1, 2, n - 1)
                subtract_blocks("GM", n, range(4, 8))
                if not first:
                    add_pair(i * 2 - 1)
                subtract_blocks("GM", n, range(8, 12))
                add_bias(i + (MOD_FIRST + IN_STEPS - 1))
                residual_pair(i * 2, 0, n + 7)
                subtract_blocks("GM", n, range(12, 15))
                add_pair(i * 2)
                subtract_blocks("GM", n, range(15, 16))

            out_step(N_OUT, 0, True)
            with dve.Fori(1, OUT_STEPS) as i:
                own.enter(i - 1, 2)
                out_step(i * 16 + N_OUT, i, False)
                own.leave(OUT_STEPS - 1)

            def up_pair(chunk, pair, bank, n_done):
                dve.wait_ge(block_done, n_done)
                dve.wait_ge(silu_done, chunk * 2 + (pair + 1))
                tiles = silu_g[:, 2 * pair:2 * pair + 2, :]
                dve.tensor_tensor(tiles, tiles, banks(bank), ALU.mult).then_inc(h_full, 1)

            def low_h(chunk, pair):
                dve.wait_ge(h_hi_ready, chunk * 2 + (pair + 1))
                tiles = slice(2 * pair, 2 * pair + 2)
                dve.tensor_tensor(h_lo[:, tiles, :], silu_g[:, tiles, :], h_hi[:, tiles, :].bitcast(F32),
                                  ALU.subtract).then_inc(h_ready, 1)

            def down_pair(j, n_done):
                dve.wait_ge(block_done, n_done)
                for a in range(2):
                    k = 2 * j + a
                    for seg, start, end in SEGMENTS:
                        last = dve.scalar_tensor_tensor(
                            xT[:, k, start:end], psum[:, DOWN_BANKS[j] + a, start:end],
                            modT[:, 5 * KT + k, seg:seg + 1], xT[:, k, start:end], ALU.mult, ALU.add)
                last.then_inc(down_drained, 1)

            subtract_blocks("GM", N_G0, range(0, 4))
            copy_row(None, N_G0)
            residual_pair(KT // 2 - 1, 2, N_G0 - 1)
            add_bias(MOD_STEPS - 3)
            dve.wait_ge(mod_ready, MOD_STEPS - 2)
            dve.wait_ge(x1_ready, KT // 2)
            make_gain(1, 4)
            add_pair(KT // 2 - 1)
            make_rstd(1)
            norm_tiles(1, 3)
            subtract_blocks("GM", N_G0, range(4, 16))
            subtract_blocks("GM", N_U0, range(0, 4))
            copy_row(None, N_U0)
            subtract_blocks("GM", N_U0, range(4, 12))
            add_bias(MOD_STEPS - 2)
            up_pair(0, 0, UP_BANKS[0], N_U0 + 7)
            subtract_blocks("GM", N_U0, range(12, 14))
            low_h(0, 0)
            subtract_blocks("GM", N_U0, range(14, 16))
            subtract_blocks("G", N_G1, range(0, 4))
            copy_row(None, N_G1)
            up_pair(0, 1, FIRST_UP_BANKS[1], N_G1 - 1)
            subtract_blocks("G", N_G1, range(4, 5))
            low_h(0, 1)
            subtract_blocks("G", N_G1, range(5, 8))
            add_bias(MOD_STEPS - 1)
            dve.wait_ge(mod_ready, MOD_STEPS)

            def down_up_steps(n, chunk):
                subtract_blocks("D", n, range(0, 4))
                for j in range(4):
                    subtract_blocks("D", n, range(4 + j, 5 + j))
                    down_pair(j, n + j + 1)
                for j in range(4):
                    subtract_blocks("G", n + 8, range(j, j + 1))
                    down_pair(4 + j, n + j + 5)
                dve.wait_ge(down_drained, chunk * 8 + 8)
                subtract_blocks("G", n + 8, range(4, 8))
                up_pair(chunk + 1, 0, UP_BANKS[0], n + 8 + 4)

            with dve.Fori(0, TURNS) as i:
                n = i * PER_CHUNK + N_LOOP
                down_up_steps(n, i)
                subtract_blocks("G", n + 16, range(0, 1))
                low_h(i + 1, 0)
                subtract_blocks("G", n + 16, range(1, 4))
                up_pair(i + 1, 1, UP_BANKS[1], n + 16)
                subtract_blocks("G", n + 16, range(4, 5))
                low_h(i + 1, 1)
                subtract_blocks("G", n + 16, range(5, 8))
            down_up_steps(N_D, CHUNKS - 2)
            subtract_blocks("D", N_D + 16, range(0, 1))
            low_h(CHUNKS - 1, 0)
            subtract_blocks("D", N_D + 16, range(1, 4))
            up_pair(CHUNKS - 1, 1, UP_BANKS[1], N_D + 16)
            low_h(CHUNKS - 1, 1)
            then(dve.memset(sumsq[:], 0.0))

            def last_squares(pair):
                count = KT + KT // 2 + pair + 1
                dve.wait_ge(squared, count)
                then(dve.tensor_tensor(sumsq[:], sumsq[:], squares[:, 0, :], ALU.add))
                dve.tensor_tensor(sumsq[:], sumsq[:], squares[:, 1, :], ALU.add).then_inc(summed, 1)
                dve.wait_ge(summed, count)

            for j in range(8):
                if j < 4:
                    subtract_blocks("D", N_D + 16, range(4 + j, 5 + j))
                down_pair(j, N_D + 16 + j + 1)
                if j:
                    last_squares(j - 1)
            last_squares(7)
            make_rstd(2)
            dve.wait_ge(down_drained, 8 * CHUNKS)
            for g in range(4):
                if g >= 2:
                    dve.wait_ge(y_turned, g - 1)
                for a in range(4):
                    k = 4 * g + a
                    at = column["final_g"] + k
                    last = dve.scalar_tensor_tensor(y_tiles[g % 2][:, a, :], xT[:, k, :], prm[:, at:at + 1],
                                                    rstd[:], ALU.mult, ALU.mult)
                last.then_inc(y_ready, 1)

        @block_ctx.tensor
        def _(pe):
            def product(bank, hi, lo, x_hi, x_lo, first, last):
                pe.matmul(psum[:, bank, 0:T], hi, x_hi, start=first, stop=False)
                pe.matmul(psum[:, bank, 0:T], hi, x_lo, start=False, stop=False)
                return pe.matmul(psum[:, bank, 0:T], lo, x_hi, start=False, stop=last)

            def gemm_block(n, kind, b, bank, x_hi, x_lo, k0, first, last, acts=None):
                pe.wait_ge(lo_ready, n + 1)
                hi, lo = split_view(w_hi, kind, b), split_view(w_lo, kind, b)
                for kk in range(4):
                    if acts is not None and kk % 2 == 0:
                        pe.wait_ge(act_ready, acts + kk // 2)
                    for o in range(2):
                        out = product(bank + o, hi[:, kk, o * P:(o + 1) * P], lo[:, kk, o * P:(o + 1) * P],
                                      x_hi[:, k0 + kk, :], x_lo[:, k0 + kk, :],
                                      first and kk == 0, last and kk == 3)
                out.then_inc(block_done, 1)

            def mod_block(n, kind, b, k0):
                pe.wait_ge(lo_ready, n + 1)
                hi, lo = split_view(w_hi, kind, b), split_view(w_lo, kind, b)
                for kk in range(2):
                    k = k0 + kk
                    pe.matmul(psum[0:4, MOD_BANK, :], cond_w[:, k, :], hi[:, kk, :], start=k == 0, stop=False)
                    out = pe.matmul(psum[0:4, MOD_BANK, :], cond_w[:, k, :], lo[:, kk, :], start=False,
                                    stop=k == KT - 1)
                out.then_inc(block_done, 1)

            def turn_row(m):
                pe.wait_ge(row_ready, m + 1)
                if not isinstance(m, int) or m:
                    pe.wait_ge(mod_ready, m)
                for a in range(4):
                    out = pe.matmul(psum[:, SMALL_BANK, 2 * a:2 * a + 2], mod_row[:, a * P:(a + 1) * P], select[:],
                                    start=True, stop=True)
                out.then_inc(row_turned, 1)

            def gm_step(n, m, bank_free, acts=None, k_order=(0, 1), turn_at=5, gates=None, pair_banks=(0, 2)):
                for b in range(16):
                    pair, j = b // 8, (b % 8) // 2
                    if b == turn_at:
                        turn_row(m - 1)
                    if gates is not None and b % 8 == 0:
                        gates(pair)
                    if b % 2 == 0:
                        if j == 0:
                            bank_free(pair)
                        gemm_block(n + b, "GM", b, pair_banks[pair], act_hi, act_lo,
                                   8 * k_order[j // 2] + 4 * (j % 2), j == 0, j == 3,
                                   acts + 2 * j + 1 if acts is not None and pair == 0 else None)
                    else:
                        if b == 1:
                            pe.wait_ge(row_ready, m)
                        mod_block(n + b, "GM", b, 2 * (b // 2))

            pe.wait_ge(tables_landed, 48)
            pe.wait_ge(params_landed, 16 * len(sizes))
            for g, group in enumerate(groups):
                rows = sum(r for _, r in group)
                pe.transpose(psum[:, SMALL_BANK, g * P:g * P + rows], prm_rows[0:rows, g, :], ident[0:rows, 0:rows])\
                    .then_inc(turned, 1)
            pe.wait_ge(x_landed, 48)
            for k in range(KT):
                if k >= 4:
                    pe.wait_ge(x_ready, k - 3)
                for a in range(3):
                    out = pe.transpose(psum[:, k % 4, a * P:(a + 1) * P], x_rows[:, a, k * P:(k + 1) * P], ident[:])
                out.then_inc(x_turned, 1)
            pe.wait_ge(summed, KT)
            pe.wait_ge(zeroed, 2)
            pe.wait_ge(prm_ready, 3)
            pe.matmul(psum[:, SMALL_BANK, 0:T], ones[:], sumsq[:], start=True, stop=True).then_inc(sum_done, 1)
            pe.wait_ge(cond_ready, 1)
            pe.wait_ge(root_ready, 1)
            def mod_step(m):
                if not isinstance(m, int) or m:
                    pe.wait_ge(row_ready, m)
                for b in range(8):
                    mod_block(m * 8 + b, "M", b, 2 * b)
                    if b == 4 and (not isinstance(m, int) or m):
                        turn_row(m - 1)

            mod_step(0)
            mod_step(1)
            with pe.Fori(2, MOD_FIRST) as i:
                mod_step(i)

            def head_gates(head, direction):
                if direction == 0:
                    pe.wait_ge(gate_w_landed, head * 32 + 32)
                    pe.wait_ge(xc_ready, head + 1)
                if direction or not isinstance(head, int) or head:
                    pe.wait_ge(gates_read, head * 2 + direction)
                for bank, which in ((R_BANK, direction), (I_BANK, 2 + direction)):
                    out = pe.matmul(psum[:, bank, 0:T], gate_w[:, which, :],
                                    mix[:, bass.ds(head, 1), :].rearrange("p a t -> p (a t)"), start=True, stop=True)
                out.then_inc(gates_done, 1)

            pairs = KT // 2
            gm_step(N_IN, MOD_FIRST, lambda pair: None, acts=0, turn_at=0)
            gm_step(N_IN + 16, MOD_FIRST + 1, lambda pair: pe.wait_ge(padded_ready, 2 * pair + 2))
            gm_step(N_IN + 32, MOD_FIRST + 2, lambda pair: pe.wait_ge(padded_ready, 2 * pair + 6),
                    gates=lambda direction: head_gates(0, direction))
            with pe.Fori(3, IN_STEPS) as i:
                gm_step(i * 16 + N_IN, i + MOD_FIRST, lambda pair: pe.wait_ge(drained, i * 2 + (pair - 5)),
                        gates=lambda direction: head_gates(i - FIRST_LRU, direction))
            gm_step(N_OUT, MOD_FIRST + IN_STEPS, lambda pair: pe.wait_ge(drained, 2 * IN_STEPS + pair - 5),
                    acts=pairs, k_order=(1, 0))
            with pe.Fori(1, OUT_STEPS) as i:
                gm_step(i * 16 + N_OUT, i + (MOD_FIRST + IN_STEPS), lambda pair: pe.wait_ge(x1_ready, i * 2 + (pair - 1)),
                        k_order=(1, 0))

            def sum_channels(which, count):
                pe.wait_ge(summed, count)
                pe.matmul(psum[:, SMALL_BANK, 0:T], ones[:], sumsq[:], start=True, stop=True).then_inc(sum_done, 1)
                pe.wait_ge(root_ready, which + 1)

            def g_step(n, pair_banks, bank_free, turn=False):
                for b in range(8):
                    if b % 4 == 0:
                        bank_free(b // 4)
                    gemm_block(n + b, "G", b, pair_banks[b // 4], act_hi, act_lo, 4 * (b % 4), b % 4 == 0, b % 4 == 3)
                    if turn and b == 3:
                        turn_row(MOD_STEPS - 1)

            def d_step(n, chunk, last=False):
                pe.wait_ge(h_ready, chunk * 2 + 2)
                for b in range(8):
                    if b in (2, 3):
                        if last:
                            pe.wait_ge(down_drained, chunk * 8 + (b - 3))
                        else:
                            pe.wait_ge(silu_done, chunk * 2 + (b + 1))
                    if b >= 4:
                        pe.wait_ge(down_drained, chunk * 8 + (b - 3))
                    gemm_block(n + b, "D", b, DOWN_BANKS[b], h_hi, h_lo, 0, True, True)

            turn_row(MOD_STEPS - 3)
            pe.wait_ge(mod_ready, MOD_STEPS - 2)
            sum_channels(1, KT + KT // 2)
            gm_step(N_G0, MOD_STEPS - 2, lambda pair: pe.wait_ge(x1_ready, 2 * OUT_STEPS - 1 + pair),
                    acts=2 * pairs, turn_at=None)
            gm_step(N_U0, MOD_STEPS - 1, lambda pair: pe.wait_ge(silu_done, 2) if pair else None,
                    pair_banks=FIRST_UP_BANKS)
            pe.wait_ge(silu_done, 1)
            g_step(N_G1, (0, 2), lambda pair: pe.wait_ge(h_full, 2) if pair else None, turn=True)
            pe.wait_ge(mod_ready, MOD_STEPS)
            with pe.Fori(0, TURNS) as i:
                n = i * PER_CHUNK + N_LOOP
                d_step(n, i)
                g_step(n + 8, UP_BANKS, lambda pair: pe.wait_ge(down_drained, i * 8 + (pair + 5)))
                g_step(n + 16, (0, 2), lambda pair: pe.wait_ge(down_drained, i * 8 + (pair + 7)))
            d_step(N_D, CHUNKS - 2)
            g_step(N_D + 8, UP_BANKS, lambda pair: pe.wait_ge(down_drained, 8 * (CHUNKS - 2) + pair + 5))
            d_step(N_D + 16, CHUNKS - 1, last=True)

            sum_channels(2, KT + 2 * (KT // 2))
            pe.transpose(psum[0:2 * HEADS, SMALL_BANK, 0:P], stateT[:], ident[:]).then_inc(state_turned, 1)
            for g in range(4):
                pe.wait_ge(y_ready, g + 1)
                if g >= 2:
                    pe.wait_ge(y_copied, g - 1)
                for k in range(4):
                    for a in range(3):
                        out = pe.transpose(psum[:, 3 * (g % 2) + a, k * P:(k + 1) * P],
                                           y_tiles[g % 2][:, k, a * P:(a + 1) * P], ident[:])
                out.then_inc(y_turned, 1)


INPUTS = ["x_prompt", "x_sample", "state_rglru", "c", "c_ctx", "w_mod", "b_mod", "norm_g", "w_in", "lru_conv_w",
          "lru_conv_b", "lru_w_a", "lru_b_a", "lru_w_i", "lru_b_i", "lru_lambda", "sc_conv_w", "w_out", "w_gate",
          "w_up", "w_down", "final_g"]


def shape_tables(d_model, tokens):
    n_freq = d_model // 4
    freqs = np.float32(1.0) / np.float32(POS_BASE) ** (np.arange(n_freq, dtype=np.float32) / np.float32(n_freq))
    parts = []
    for count in (tokens // GRID_W, GRID_W):
        angle = freqs[:, None] * np.arange(count, dtype=np.float32)
        both = np.concatenate([np.sin(angle), np.cos(angle)]).reshape(-1, P, count)
        parts.append(both.transpose(1, 0, 2).reshape(P, -1))
    pick = np.zeros((P, 2), np.float32)
    pick[np.arange(4), np.arange(4) % 2] = 1.0
    return np.ascontiguousarray(np.concatenate(parts + [np.eye(P), pick], 1), np.float32)


def kernel(**inputs):
    import concourse.bacc as bacc
    from concourse.bass_utils import run_bass_kernel_spmd

    nc = bacc.Bacc("TRN2", target_bir_lowering=False, num_devices=1)
    arrays = {name: np.ascontiguousarray(inputs[name]) for name in INPUTS}
    arrays["tables"] = shape_tables(arrays["x_sample"].shape[2], arrays["x_sample"].shape[1])
    args = [nc.dram_tensor(f"in_{name}", a.shape, mybir.dt.from_np(a.dtype), kind="ExternalInput").ap()
            for name, a in arrays.items()]
    batch, _, _, width = arrays["state_rglru"].shape
    outputs = {"y_prompt": arrays["x_prompt"].shape, "y_sample": arrays["x_sample"].shape,
               "new_state": (arrays["x_prompt"].shape[0], arrays["state_rglru"].shape[1], 2, width)}
    args += [nc.dram_tensor(name, shape, F32, kind="ExternalOutput").ap() for name, shape in outputs.items()]
    build(nc, *args)
    result = run_bass_kernel_spmd(nc, [{f"in_{name}": a for name, a in arrays.items()}], core_ids=[0])
    return tuple(result.results[0][name] for name in outputs)
```

```python
from contextlib import ExitStack

import concourse.bass as bass
import numpy as np
from concourse import mybir

ALU = mybir.AluOpType
ACT = mybir.ActivationFunctionType
F32 = mybir.dt.float32
F32R = mybir.dt.float32r

P = 128
SLOTS = 4
BLOCK = 1024
BANK = 512
EPS = 1e-6
LRU_C = 8.0
GRID_W = 64
POS_BASE = 10000.0
ATANH_TERMS = [1.0 / n for n in range(17, 1, -2)]


class Tally:

    def __init__(self, sem):
        self.sem, self.base, self.added = sem, 0, 0

    @property
    def value(self):
        return self.base + self.added

    def add(self, instruction):
        instruction.then_inc(self.sem, 1)
        self.added += 1

    def enter(self, i, per_turn):
        self.start, self.per_turn = self.value, per_turn
        self.base, self.added = i * per_turn + self.start, 0

    def leave(self, turns):
        assert self.added == self.per_turn, (self.added, self.per_turn)
        self.base, self.added = self.start + turns * self.per_turn, 0


def build(nc, x_prompt, x_sample, state_rglru, c, c_ctx, w_mod, b_mod, norm_g, w_in, lru_conv_w, lru_conv_b,
          lru_w_a, lru_b_a, lru_w_i, lru_b_i, lru_lambda, sc_conv_w, w_out, w_gate, w_up, w_down, final_g,
          tables, y_prompt, y_sample, new_state):
    D = x_prompt.shape[2]
    CTX = x_prompt.shape[1]
    SMP = x_sample.shape[1]
    T = CTX + SMP
    KT = D // P
    W = lru_lambda.shape[2]
    HEADS = W // P
    FF = w_gate.shape[2]
    GRID_ROWS = SMP // GRID_W
    CHUNK = 4
    CHUNKS = FF // P // CHUNK
    assert CTX == P and SMP == 2 * P and W == 8 * P and D == 2 * W and FF % (CHUNK * P) == 0
    CONV, SC = lru_conv_w.shape[1], sc_conv_w.shape[1]
    SEGMENTS = ((0, 0, CTX), (1, CTX, T))

    PAD = 2
    CTX_AT, SMP_AT = PAD, PAD + CTX + PAD
    PADDED = SMP_AT + SMP + PAD
    RUN = SMP_AT - PAD + SMP

    sizes = [("ctx_c", KT), ("c", KT), ("norm_g", 2 * KT), ("state", 2 * HEADS), ("b_a", 2 * HEADS),
             ("b_i", 2 * HEADS), ("lam", 2 * HEADS),
             ("b_mod", 6 * KT), ("final_g", KT), ("conv_b", HEADS),
             ("conv_w", CONV * HEADS), ("sc_w", SC * HEADS)]
    sources = dict(ctx_c=c_ctx, c=c[0], norm_g=norm_g[0].rearrange("a d -> (a d)"),
                   state=state_rglru[0, 0].rearrange("a d -> (a d)"),
                   b_a=lru_b_a[0].rearrange("a h e -> (a h e)"), b_i=lru_b_i[0].rearrange("a h e -> (a h e)"),
                   lam=lru_lambda[0].rearrange("a d -> (a d)"), b_mod=b_mod[0], final_g=final_g,
                   conv_b=lru_conv_b[0], conv_w=lru_conv_w[0].rearrange("a d -> (a d)"),
                   sc_w=sc_conv_w[0].rearrange("a d -> (a d)"))
    groups = [sizes[:2], sizes[2:7], sizes[7:10], sizes[10:]]
    at, column = 0, {}
    for name, rows in sizes:
        column[name] = at
        at += rows
    PARAMS = at

    MOD_FIRST = 2 * D // 512
    MOD_STEPS = 6 * D // 512
    IN_STEPS, OUT_STEPS = w_in.shape[2] // 512, D // 512
    assert MOD_STEPS - MOD_FIRST == IN_STEPS + OUT_STEPS + 2
    N_IN = MOD_FIRST * 8
    N_OUT = N_IN + IN_STEPS * 16
    N_G0 = N_OUT + OUT_STEPS * 16
    N_U0 = N_G0 + 16
    N_G1 = N_U0 + 16
    N_LOOP = N_G1 + 8
    PER_CHUNK = 24
    TURNS = CHUNKS - 2
    N_D = N_LOOP + TURNS * PER_CHUNK
    PHASES = [("x", 0), ("c", 2 * W + W), ("v", 2 * W + 2 * W), ("b", 2 * W), ("y", W)]
    FIRST_LRU = 2

    with ExitStack() as ctx:
        def sb(name, shape, dt=F32):
            return ctx.enter_context(nc.sbuf_tensor(name, shape, dt))

        def sem(name):
            return ctx.enter_context(nc.semaphore(name))

        xT = sb("xT", [P, KT, T])
        act_hi = sb("act_hi", [P, KT, T], F32R)
        act_lo = sb("act_lo", [P, KT, T], F32R)
        stage = sb("stage", [P, KT * T])
        raw = [sb(f"raw{s}", [P, 2 * BLOCK]) for s in range(SLOTS)]
        w_hi = [sb(f"w_hi{s}", [P, BLOCK], F32R) for s in range(SLOTS)]
        w_lo = [sb(f"w_lo{s}", [P, BLOCK], F32R) for s in range(SLOTS)]
        h_hi = sb("h_hi", [P, CHUNK, T], F32R)
        h_lo = sb("h_lo", [P, CHUNK, T], F32R)
        scratch = sb("scratch", [P, 8 * T + 4 * PADDED + 2 * T])
        sumsq = sb("sumsq", [P, T])
        rstd = sb("rstd", [P, T])
        gate_w = sb("gate_w", [P, 4, P])
        mod_row = sb("mod_row", [4, BANK])
        prm = sb("prm", [P, PARAMS])
        modT = sb("modT", [P, 6 * KT, 2])
        gain = sb("gain", [P, 2, KT, 2])
        cond = sb("cond", [P, 2, KT])
        cond_w = sb("cond_w", [P, KT, 4], F32R)
        decay = sb("decay", [P, 3, 2 * HEADS])
        stateT = sb("stateT", [P, 2 * HEADS])
        ident = sb("ident", [P, P])
        ones = sb("ones", [P, P])
        eps = sb("eps", [P, 1])
        token_rstd = sb("token_rstd", [P, 3])
        state_rows = sb("state_rows", [2 * HEADS, P])
        select = sb("select", [4, 2])

        x_rows = stage[:].rearrange("p (a d) -> p a d", a=3)
        mix = stage[:].rearrange("p (k t) -> p k t", k=KT)
        silu_g = mix[:, 0:CHUNK, :]
        lru = scratch[:, 0:8 * T].rearrange("p (b d t) -> p b d t", b=4, d=2)
        gate_r, gate_i, decay_t, decay_a = (lru[:, b] for b in range(4))
        normed = [lru[:, b] for b in (0, 1)]
        scaled = [lru[:, b] for b in (2, 3)]
        y_tiles = [scratch[:, b * 2 * T:(b + 1) * 2 * T].rearrange("p (k t) -> p k t", k=2) for b in (0, 1)]
        conv_rows = scratch[:, 8 * T:8 * T + 4 * PADDED].rearrange("p (b n) -> p b n", b=4)
        padded, conv_sum = conv_rows[:, 0:2, :], conv_rows[:, 2:4, :]
        squares = scratch[:, 8 * T:10 * T].rearrange("p (a t) -> p a t", a=2)
        x_squares = scratch[:, 4 * T:8 * T].rearrange("p (a t) -> p a t", a=4)
        last_squares = [scratch[:, (4 + 2 * b) * T:(6 + 2 * b) * T].rearrange("p (k t) -> p k t", k=2) for b in (0, 1)]
        gelu_y = scratch[:, 8 * T + 4 * PADDED:].rearrange("p (a t) -> p a t", a=2)
        prm_rows = scratch[:, 0:4 * P].rearrange("p (g n) -> p g n", g=4)
        small = scratch[:, 4 * P:4 * P + 8 * 2 * HEADS].rearrange("p (a n) -> p a n", a=8)
        POS = GRID_ROWS * (KT // 2) + GRID_W * (KT // 2)
        pos = scratch[:, 8 * T + 2 * T:8 * T + 2 * T + POS]
        pos_row = pos[:, 0:GRID_ROWS * (KT // 2)].rearrange("p (k r) -> p k r", r=GRID_ROWS)
        pos_col = pos[:, GRID_ROWS * (KT // 2):POS].rearrange("p (k w) -> p k w", w=GRID_W)

        psum = ctx.enter_context(nc.psum_tensor("psum", [P, 8, BANK], F32))
        R_BANK, I_BANK, MOD_BANK, SMALL_BANK = 4, 5, 6, 7
        SUM_BANK = 5
        UP_BANKS, FIRST_UP_BANKS = (4, 6), (4, 2)
        DOWN_BANKS = (4, 6, 0, 2, 4, 6, 0, 2)
        LAST_DOWN_BANKS = (4, 6, 4, 6, 4, 6, 4, 6)
        TOKEN_BANK, STATE_BANK = 3, 4

        def turned_pair(pair):
            return psum[:, 0:3, 256 * (pair % 2):256 * (pair % 2) + 256]

        def y_rows(pair):
            return x_rows[:, :, 2 * P * pair:2 * P * (pair + 1)]

        V_DRAINED, B_DRAINED, Y_DRAINED = HEADS // 2, 2 * (HEADS // 2), 3 * (HEADS // 2)

        def banks(b, n=2):
            return psum[:, b:b + n, 0:T]

        tables_landed = sem("tables_landed")
        params_landed = sem("params_landed")
        x_landed = sem("x_landed")
        gate_w_landed = sem("gate_w_landed")
        landed = [sem(f"landed{s}") for s in range(SLOTS)]
        hi_ready = sem("hi_ready")
        lo_ready = sem("lo_ready")
        block_done = sem("block_done")
        zeroed = sem("zeroed")
        turned = sem("turned")
        prm_ready = sem("prm_ready")
        silu_ready = sem("silu_ready")
        exp_lam_ready = sem("exp_lam_ready")
        abs_ready = sem("abs_ready")
        cond_hi_ready = sem("cond_hi_ready")
        cond_ready = sem("cond_ready")
        decay_ready = sem("decay_ready")
        cond_landed = sem("cond_landed")
        x_turned = sem("x_turned")
        ctx_copied = sem("ctx_copied")
        x_ready = sem("x_ready")
        hat_ready = sem("hat_ready")
        squared = sem("squared")
        summed = sem("summed")
        sum_done = sem("sum_done")
        root_ready = sem("root_ready")
        normed_ready = sem("normed_ready")
        scaled_ready = sem("scaled_ready")
        act_hi_ready = sem("act_hi_ready")
        act_ready = sem("act_ready")
        row_ready = sem("row_ready")
        row_turned = sem("row_turned")
        mod_ready = sem("mod_ready")
        drained = sem("drained")
        padded_ready = sem("padded_ready")
        xc_ready = sem("xc_ready")
        gates_done = sem("gates_done")
        gates_read = sem("gates_read")
        decays_ready = sem("decays_ready")
        power_ready = sem("power_ready")
        root_u_ready = sem("root_u_ready")
        head_done = sem("head_done")
        gelu_ready = sem("gelu_ready")
        x1_ready = sem("x1_ready")
        silu_done = sem("silu_done")
        h_full = sem("h_full")
        h_hi_ready = sem("h_hi_ready")
        h_ready = sem("h_ready")
        down_drained = sem("down_drained")
        y_ready = sem("y_ready")
        y_turned = sem("y_turned")
        y_copied = sem("y_copied")
        y_done = sem("y_done")
        y_act_done = sem("y_act_done")
        state_turned = sem("state_turned")
        state_copied = sem("state_copied")
        rstd_ready = sem("rstd_ready")
        dve_step = sem("dve_step")
        stored = sem("stored")

        w_mod_v = w_mod[0].rearrange("(k p) n -> p k n", p=P)
        w_in_v = w_in[0].rearrange("(k p) n -> p k n", p=P)
        w_out_v = w_out[0].rearrange("(k p) n -> p k n", p=P)
        w_gate_v = w_gate[0].rearrange("(k p) n -> p k n", p=P)
        w_up_v = w_up[0].rearrange("(k p) n -> p k n", p=P)
        w_down_v = w_down[0].rearrange("(k p) n -> p k n", p=P)

        def slot_of(block):
            return block % SLOTS

        def raw_of(kind, block):
            if kind == "GM":
                quad, at = divmod(block, 4)
                half, second = at % 2, at // 2
                wide = half == 1
            else:
                quad, at = divmod(block, 4)
                half, second = divmod(at, 2)
                wide = kind != "G"
            slot = 2 * (quad % 2) + half
            if not wide:
                return slot, raw[slot][:].rearrange("p (k n) -> p k n", n=256)[:, 4 * second:4 * second + 4, :]
            view = raw[slot][:].rearrange("p (k n) -> p k n", n=512)
            if kind == "D":
                return slot, view[:, :, 256 * second:256 * second + 256]
            return slot, view[:, 2 * second:2 * second + 2, :]

        def split_view(tile, kind, block):
            n = 512 if kind == "M" or (kind == "GM" and block % 2) else 256
            return tile[slot_of(block)][:].rearrange("p (k n) -> p k n", n=n)

        def landed_by(n, block):
            return (n - block) * 2 + 16 * (block // 8) + 16

        block_ctx = ctx.enter_context(nc.Block())

        @block_ctx.sync
        def _(sp):
            def quad(n, quad_at, halves, apart=False):
                first = 2 * (quad_at % 2)
                for half, source in enumerate(halves):
                    if not isinstance(n, int) or n >= 8:
                        sp.wait_ge(lo_ready, n - 6 + 2 * half if apart else n - 4)
                    width = source.shape[2]
                    sp.dma_start(raw[first + half][:].rearrange("p (k n) -> p k n", n=width), source)\
                        .then_inc(landed[first + half], 16)

            def held(value):
                return value if isinstance(value, int) else sp.snap(value)

            def mod_half(at, quarter):
                return w_mod_v[:, 4 * quarter:4 * quarter + 4, bass.ds(at, 512)]

            def g_half(view, col, quad_at, k_order=(0, 1)):
                k = 8 * k_order[quad_at % 2]
                return view[:, k:k + 8, bass.ds(col + 256 * (quad_at // 2), 256)]

            def gm_step(n, view, col, m, k_order=(0, 1)):
                at = held(m * 512)
                for q in range(4):
                    quad(n + 4 * q, q, [g_half(view, col, q, k_order), mod_half(at, q)])

            def g_step(n, view, col, apart=True):
                col = held(col)
                for q in range(2):
                    quad(n + 4 * q, q, [g_half(view, col, 2 * q), g_half(view, col, 2 * q + 1)], apart=apart)

            def d_step(n, chunk):
                first_k = held(chunk * CHUNK)
                for q in range(2):
                    quad(n + 4 * q, q, [w_down_v[:, bass.ds(first_k, CHUNK), 1024 * q + 512 * h:1024 * q + 512 * h + 512]
                                        for h in range(2)], apart=True)

            def m_step(n, m):
                at = held(m * 512)
                for q in range(2):
                    quad(n + 4 * q, q, [mod_half(at, 2 * q), mod_half(at, 2 * q + 1)], apart=True)

            m_step(0, 0)
            sp.dma_start(x_rows[:, 0, :], x_prompt[0]).then_inc(x_landed, 16)
            for a in range(2):
                sp.dma_start(x_rows[:, 1 + a, :], x_sample[0, a * P:(a + 1) * P, :]).then_inc(x_landed, 16)
            with sp.Fori(1, MOD_FIRST) as i:
                m_step(i * 8, i)
            for phase, (_, col) in enumerate(PHASES):
                with sp.Fori(0, 2) as i:
                    gm_step(i * 16 + N_IN + 32 * phase, w_in_v, i * 512 + col, i + (MOD_FIRST + 2 * phase))
            with sp.Fori(1, OUT_STEPS + 1) as i:
                gm_step(i * 16 + (N_OUT - 16), w_out_v, i * 512 - 512, i + (MOD_FIRST + IN_STEPS - 1), k_order=(1, 0))
            gm_step(N_G0, w_gate_v, 0, MOD_STEPS - 2)
            gm_step(N_U0, w_up_v, 0, MOD_STEPS - 1)
            g_step(N_G1, w_gate_v, 512, apart=False)
            with sp.Fori(0, TURNS) as i:
                n = i * PER_CHUNK + N_LOOP
                d_step(n, i)
                g_step(n + 8, w_up_v, i * 512 + 512)
                g_step(n + 16, w_gate_v, i * 512 + 1024)
            d_step(N_D, CHUNKS - 2)
            g_step(N_D + 8, w_up_v, (CHUNKS - 1) * 512)
            d_step(N_D + 16, CHUNKS - 1)
            for half in range(2):
                for a in range(2):
                    cols = slice(D // 2 * half, D // 2 * (half + 1))
                    sp.wait_ge(y_done, 2 * half + a + 1)
                    to = (y_prompt[0], y_sample[0, 0:P])[a]
                    sp.dma_start(to[:, cols], x_rows[:, a, cols]).then_inc(stored, 16)
            for half in range(2):
                cols = slice(D // 2 * half, D // 2 * (half + 1))
                sp.wait_ge(y_act_done, half + 1)
                sp.dma_start(y_sample[0, P:2 * P, cols], x_rows[:, 2, cols]).then_inc(stored, 16)
            sp.wait_ge(state_copied, 1)
            sp.dma_start(new_state[0, 0].rearrange("a (h e) -> (a h) e", e=P), state_rows[:]).then_inc(stored, 16)
            sp.wait_ge(stored, 16 * 7)

        @block_ctx.gpsimd
        def _(pool):
            for g, group in enumerate(groups[1:], 1):
                row = 0
                for name, rows in group:
                    pool.dma_start(prm_rows[row:row + rows, g, :], sources[name].rearrange("(r e) -> r e", e=P))\
                        .then_inc(params_landed, 16)
                    row += rows
            pool.dma_start(pos, tables[:, 0:POS]).then_inc(tables_landed, 16)
            pool.dma_start(select[:], tables[0:4, POS + P:POS + P + 2]).then_inc(tables_landed, 16)
            pool.memset(ones[:], 1.0).then_inc(zeroed, 1)
            pool.memset(eps[:], EPS).then_inc(zeroed, 1)
            pool.wait_ge(x_ready, 4)
            pool.memset(padded, 0.0).then_inc(zeroed, 1)
            pool.wait_ge(rstd_ready, 1)
            for pair in range(KT // 2):
                tiles = slice(2 * pair, 2 * pair + 2)
                pool.tensor_tensor(mix[:, tiles, :], xT[:, tiles, :],
                                   rstd[:].rearrange("p (a t) -> p a t", a=1).broadcast_to([P, 2, T]), ALU.mult)\
                    .then_inc(hat_ready, 1)
            for h in range(HEADS):
                if h:
                    pool.wait_ge(gates_done, 2 * h)
                pool.dma_start(gate_w[:, 0:2, :], lru_w_a[0, :, h].rearrange("a d e -> d a e"))\
                    .then_inc(gate_w_landed, 16)
                pool.dma_start(gate_w[:, 2:4, :], lru_w_i[0, :, h].rearrange("a d e -> d a e"))\
                    .then_inc(gate_w_landed, 16)

        @block_ctx.scalar
        def _(act):
            def round_blocks(kind, n, blocks):
                for b in blocks:
                    slot, source = raw_of(kind, b)
                    act.wait_ge(landed[slot], landed_by(n + b, b))
                    if not isinstance(n, int) or n + b >= SLOTS:
                        act.wait_ge(block_done, n + b - (SLOTS - 1))
                    act.activation(split_view(w_hi, kind, b), source, ACT.Copy).then_inc(hi_ready, 1)

            def root_of_mean_square(which):
                act.wait_ge(sum_done, which + 4)
                act.activation(rstd[:], psum[:, SUM_BANK, 0:T], ACT.Sqrt, bias=eps[:], scale=1.0 / D)\
                    .then_inc(root_ready, 1)

            def norm_pair(which, shift, pair, source):
                b, done = pair % 2, pair + which * (KT // 2)
                act.wait_ge(normed_ready, done + 1)
                for a in range(2):
                    k = 2 * pair + a
                    shift_at = shift * KT + k
                    last = act.activation(scaled[b][:, a, CTX:T], source[:, a, CTX:T], ACT.Identity,
                                          bias=modT[:, shift_at, 1:2], scale=gain[:, which, k, 1:2])
                last.then_inc(scaled_ready, 1)
                act.wait_ge(scaled_ready, done + 1)
                act.activation(act_hi[:, 2 * pair:2 * pair + 2, :], scaled[b], ACT.Copy).then_inc(act_hi_ready, 1)

            act.dma_start(prm_rows[0:KT, 0, :], sources["ctx_c"].rearrange("(r e) -> r e", e=P)).then_inc(cond_landed, 16)
            act.dma_start(prm_rows[KT:2 * KT, 0, :], sources["c"].rearrange("(r e) -> r e", e=P)).then_inc(cond_landed, 16)
            act.dma_start(ident[:], tables[:, POS:POS + P]).then_inc(cond_landed, 16)
            act.wait_ge(prm_ready, 1)
            act.activation(cond[:], prm[:, 0:2 * KT].rearrange("p (a k) -> p a k", a=2), ACT.Silu)\
                .then_inc(silu_ready, 1)
            act.wait_ge(silu_ready, 1)
            act.activation(cond_w[:].rearrange("p k a -> p a k")[:, 0:2, :], cond[:], ACT.Copy)\
                .then_inc(cond_hi_ready, 1)
            round_blocks("M", 0, range(8))
            lam = prm[:, column["lam"]:column["lam"] + 2 * HEADS]
            act.wait_ge(prm_ready, len(groups))
            act.activation(small[:, 0, :], lam, ACT.Abs).then_inc(abs_ready, 1)
            act.wait_ge(abs_ready, 1)
            act.activation(small[:, 1, :], small[:, 0, :], ACT.Exp, scale=-1.0).then_inc(exp_lam_ready, 1)
            for m in range(1, 5):
                round_blocks("M", 8 * m, range(6))
                act.wait_ge(x_turned, m)
                act.activation(xT[:, 4 * m - 4:4 * m, 0:CTX], psum[:, 0:4, 0:CTX], ACT.Copy).then_inc(ctx_copied, 1)
                round_blocks("M", 8 * m, range(6, 8))
                act.wait_ge(x_ready, m)
                act.wait_ge(decay_ready, 3)
                if m >= 2:
                    act.wait_ge(sum_done, m - 1)
                act.activation(x_squares, xT[:, 4 * m - 4:4 * m, :], ACT.Square).then_inc(squared, 1)
            round_blocks("M", 8 * 5, range(8))
            root_of_mean_square(0)
            with act.Fori(6, MOD_FIRST) as i:
                round_blocks("M", i * 8, range(8))

            for step in range(IN_STEPS):
                n = N_IN + 16 * step
                phase = PHASES[step // 2][0]
                before = PHASES[(step - 1) // 2][0] if step else None
                head = step - FIRST_LRU

                def pad_rows(pair, bank, n_done):
                    act.wait_ge(block_done, n_done)
                    for a in range(2):
                        tile = 2 * pair + a
                        if tile >= 2:
                            act.wait_ge(xc_ready, tile - 1)
                        else:
                            act.wait_ge(zeroed, 3)
                        act.activation(padded[:, a, CTX_AT:CTX_AT + CTX], psum[:, bank + a, 0:CTX], ACT.Copy)
                        act.activation(padded[:, a, SMP_AT:SMP_AT + SMP], psum[:, bank + a, CTX:T], ACT.Copy)\
                            .then_inc(padded_ready, 1)

                def gelu(pair, bank, n_done):
                    act.wait_ge(block_done, n_done)
                    if pair:
                        act.wait_ge(drained, Y_DRAINED + pair)
                    act.activation(gelu_y, banks(bank), ACT.Gelu_apprx_tanh).then_inc(gelu_ready, 1)

                round_blocks("GM", n, range(0, 4 if step else 2))
                if step == 0:
                    for pair in range(KT // 2):
                        norm_pair(0, 0, pair, mix[:, 2 * pair:2 * pair + 2, :])
                        if pair in (1, 3, 5):
                            round_blocks("GM", n, range(pair + 1, pair + 3))
                if before == "x":
                    pad_rows(2 * step - 1, 2, n - 1)
                if before == "y":
                    gelu(2 * (step - 8) - 1, 2, n - 1)
                if step:
                    round_blocks("GM", n, range(4, 5))
                if head >= 0:
                    act.wait_ge(gates_done, 2 * head + 1)
                    if head:
                        act.wait_ge(head_done, head)
                    for bank, bias, to in ((R_BANK, "b_a", gate_r), (I_BANK, "b_i", gate_i)):
                        at_bias = column[bias] + head
                        last = act.activation(to[:, 0, :], psum[:, bank, 0:T], ACT.Sigmoid,
                                              bias=prm[:, at_bias:at_bias + 1])
                    last.then_inc(gates_read, 1)
                round_blocks("GM", n, range(5 if step else 8, 12))
                if phase == "x":
                    pad_rows(2 * step, 0, n + 7)
                if phase == "y":
                    gelu(2 * (step - 8), 0, n + 7)
                round_blocks("GM", n, range(12, 13))
                if head >= 0:
                    act.wait_ge(gates_done, 2 * head + 2)
                    for bank, bias, to in ((R_BANK, "b_a", gate_r), (I_BANK, "b_i", gate_i)):
                        at_bias = column[bias] + HEADS + head
                        last = act.activation(to[:, 1, :], psum[:, bank, 0:T], ACT.Sigmoid,
                                              bias=prm[:, at_bias:at_bias + 1])
                    last.then_inc(gates_read, 1)
                    act.wait_ge(gates_read, 2 * head + 2)
                    if head == 0:
                        act.wait_ge(decay_ready, 3)
                    for d in range(2):
                        lam_at = d * HEADS + head
                        act.activation(decay_t[:, d, :], gate_r[:, d, :], ACT.Tanh,
                                       scale=decay[:, 0, lam_at:lam_at + 1])
                    for d in range(2):
                        lam_at = d * HEADS + head
                        act.activation(decay_a[:, d, :], gate_r[:, d, :], ACT.Exp,
                                       scale=decay[:, 1, lam_at:lam_at + 1])
                        last = act.activation(gate_r[:, d, :], gate_r[:, d, :], ACT.Exp,
                                              scale=decay[:, 2, lam_at:lam_at + 1])
                    last.then_inc(decays_ready, 1)
                round_blocks("GM", n, range(13, 16))
                if head >= 0:
                    act.wait_ge(power_ready, head + 1)
                    act.activation(decay_t, decay_t, ACT.Sqrt).then_inc(root_u_ready, 1)

            def square_pair(pair):
                act.wait_ge(x1_ready, pair + 1)
                if not isinstance(pair, int) or pair:
                    act.wait_ge(summed, pair)
                act.activation(squares, xT[:, bass.ds(pair * 2, 2), :], ACT.Square).then_inc(squared, 1)

            def out_step(n, i, first):
                if first:
                    round_blocks("GM", n, range(0, 3))
                    act.wait_ge(block_done, n)
                    for j in range(KT // 2):
                        pair = (j + KT // 4) % (KT // 2)
                        if pair < KT // 4:
                            act.wait_ge(drained, Y_DRAINED + pair + 1)
                        else:
                            act.wait_ge(drained, B_DRAINED + pair - KT // 4 + 1)
                        act.activation(act_hi[:, 2 * pair:2 * pair + 2, :], mix[:, 2 * pair:2 * pair + 2, :],
                                       ACT.Copy).then_inc(act_hi_ready, 1)
                        if j == 1:
                            round_blocks("GM", n, range(3, 4))
                        if j == 3:
                            act.wait_ge(drained, Y_DRAINED + 3)
                            act.activation(gelu_y, banks(2), ACT.Gelu_apprx_tanh).then_inc(gelu_ready, 1)
                        if j in (3, 5):
                            round_blocks("GM", n, range(j + 1, j + 3))
                else:
                    round_blocks("GM", n, range(0, 4))
                    square_pair(i * 2 - 1)
                    round_blocks("GM", n, range(4, 8))
                round_blocks("GM", n, range(8, 12))
                square_pair(i * 2)
                round_blocks("GM", n, range(12, 16))

            out_step(N_OUT, 0, True)
            with act.Fori(1, OUT_STEPS) as i:
                out_step(i * 16 + N_OUT, i, False)

            def silu_pair(chunk, pair, n_done):
                act.wait_ge(block_done, n_done)
                if not isinstance(chunk, int) or chunk:
                    act.wait_ge(h_ready, chunk * 2 + (pair - 1))
                act.activation(silu_g[:, 2 * pair:2 * pair + 2, :], banks(2 * pair), ACT.Silu).then_inc(silu_done, 1)

            def round_h(chunk, pair, n_done):
                act.wait_ge(block_done, n_done)
                act.wait_ge(h_full, chunk * 2 + (pair + 1))
                act.activation(h_hi[:, 2 * pair:2 * pair + 2, :], silu_g[:, 2 * pair:2 * pair + 2, :], ACT.Copy)\
                    .then_inc(h_hi_ready, 1)

            round_blocks("GM", N_G0, range(0, 3))
            square_pair(KT // 2 - 1)
            round_blocks("GM", N_G0, range(3, 4))
            root_of_mean_square(1)
            for pair in range(KT // 2):
                norm_pair(1, 3, pair, normed[pair % 2])
                if pair in (3, 5):
                    round_blocks("GM", N_G0, range(pair + 1, pair + 3))
            round_blocks("GM", N_G0, range(8, 12))
            silu_pair(0, 0, N_G0 + 7)
            round_blocks("GM", N_G0, range(12, 16))
            round_blocks("GM", N_U0, range(0, 4))
            silu_pair(0, 1, N_G0 + 15)
            round_blocks("GM", N_U0, range(4, 13))
            round_h(0, 0, N_U0)
            round_blocks("GM", N_U0, range(13, 16))

            def gate_step(n, chunk):
                round_blocks("G", n, range(0, 4))
                round_h(chunk - 1, 1, n - 1)
                round_blocks("G", n, range(4, 8))
                silu_pair(chunk, 0, n + 4)

            def down_step(n, chunk):
                round_blocks("D", n, range(0, 4))
                silu_pair(chunk + 1, 1, n)
                round_blocks("D", n, range(4, 8))

            def up_step(n, chunk):
                round_blocks("G", n, range(0, 8))
                round_h(chunk, 0, n)

            gate_step(N_G1, 1)
            with act.Fori(0, TURNS) as i:
                n = i * PER_CHUNK + N_LOOP
                down_step(n, i)
                up_step(n + 8, i + 1)
                gate_step(n + 16, i + 2)
            down_step(N_D, CHUNKS - 2)
            up_step(N_D + 8, CHUNKS - 1)
            round_blocks("D", N_D + 16, range(0, 3))
            round_h(CHUNKS - 1, 1, N_D + 16)
            round_blocks("D", N_D + 16, range(3, 4))
            round_blocks("D", N_D + 16, range(4, 6))
            for pair in range(KT // 2):
                act.wait_ge(down_drained, 8 * (CHUNKS - 1) + pair + 1)
                if pair >= 2:
                    act.wait_ge(summed, KT // 2 + pair - 1)
                act.activation(last_squares[pair % 2], xT[:, 2 * pair:2 * pair + 2, :], ACT.Square).then_inc(squared, 1)
                if pair >= 2:
                    act.wait_ge(y_turned, pair - 1)
                for a in range(2):
                    at = column["final_g"] + 2 * pair + a
                    last = act.activation(y_tiles[pair % 2][:, a, :], xT[:, 2 * pair + a, :], ACT.Copy,
                                          scale=prm[:, at:at + 1])
                last.then_inc(y_ready, 1)
                if pair >= 1:
                    act.wait_ge(y_turned, pair)
                    act.activation(y_rows(pair - 1), turned_pair(pair - 1), ACT.Copy).then_inc(y_copied, 1)
                if pair < 2:
                    round_blocks("D", N_D + 16, range(6 + pair, 7 + pair))
            act.wait_ge(sum_done, 6)
            act.activation(token_rstd[:], psum[:, TOKEN_BANK, 0:3], ACT.Sqrt, bias=eps[:], scale=1.0 / D)\
                .then_inc(root_ready, 1)
            act.wait_ge(y_turned, KT // 2)
            act.activation(y_rows(KT // 2 - 1), turned_pair(KT // 2 - 1), ACT.Copy).then_inc(y_copied, 1)
            act.wait_ge(rstd_ready, 3)
            act.wait_ge(y_copied, KT // 2)
            for half in range(2):
                cols = slice(D // 2 * half, D // 2 * (half + 1))
                act.activation(x_rows[:, 2, cols], x_rows[:, 2, cols], ACT.Copy, scale=token_rstd[:, 2:3])\
                    .then_inc(y_act_done, 1)
            act.wait_ge(state_turned, 1)
            act.activation(state_rows[:], psum[0:2 * HEADS, STATE_BANK, 0:P], ACT.Copy).then_inc(state_copied, 1)

        @block_ctx.vector
        def _(dve):
            own = Tally(dve_step)

            def then(instruction):
                own.add(instruction)
                dve.wait_ge(own.sem, own.value)

            def subtract_blocks(kind, n, blocks):
                for b in blocks:
                    _, source = raw_of(kind, b)
                    dve.wait_ge(hi_ready, n + b + 1)
                    dve.tensor_tensor(split_view(w_lo, kind, b), source, split_view(w_hi, kind, b).bitcast(F32),
                                      ALU.subtract).then_inc(lo_ready, 1)

            def copy_row(m, n_done):
                dve.wait_ge(block_done, n_done)
                dve.tensor_copy(mod_row[:], psum[0:4, MOD_BANK, :]).then_inc(row_ready, 1)

            def add_bias(m):
                dve.wait_ge(row_turned, m + 1)
                at = column["b_mod"]
                dve.tensor_tensor(modT[:, bass.ds(m * 4, 4), :],
                                  psum[:, SMALL_BANK, 0:8].rearrange("p (k a) -> p k a", a=2),
                                  prm[:, bass.ds(m * 4 + at, 4)].rearrange("p (k a) -> p k a", a=1)
                                  .broadcast_to([P, 4, 2]), ALU.add).then_inc(mod_ready, 1)

            def make_gain(which, scale):
                at = column["norm_g"] + which * KT
                for a in range(2):
                    last = dve.scalar_tensor_tensor(gain[:, which, :, a], modT[:, scale * KT:(scale + 1) * KT, a],
                                                    1.0, prm[:, at:at + KT], ALU.add, ALU.mult)
                then(last)

            def make_rstd(which):
                dve.wait_ge(root_ready, which + 1)
                dve.reciprocal(rstd[:], rstd[:]).then_inc(rstd_ready, 1)
                dve.wait_ge(rstd_ready, which + 1)

            def norm_tiles(which, shift, n, between):
                pairs = KT // 2
                rstd2 = rstd[:].rearrange("p (a t) -> p a t", a=1).broadcast_to([P, 2, T])

                def scale_pair(pair):
                    b = pair % 2
                    source = mix[:, 2 * pair:2 * pair + 2, :] if which == 0 else normed[b]
                    if which:
                        then(dve.tensor_tensor(source, xT[:, 2 * pair:2 * pair + 2, :], rstd2, ALU.mult))
                    for a in range(2):
                        k = 2 * pair + a
                        shift_at = shift * KT + k
                        last = dve.tensor_scalar(scaled[b][:, a, 0:CTX], source[:, a, 0:CTX],
                                                 gain[:, which, k, 0:1], modT[:, shift_at, 0:1],
                                                 ALU.mult, ALU.add)
                    last.then_inc(normed_ready, 1)

                if which == 0:
                    dve.wait_ge(hat_ready, pairs)
                scale_pair(0)
                scale_pair(1)
                for pair in range(pairs):
                    dve.wait_ge(act_hi_ready, pair + 1 + which * 2 * pairs)
                    dve.tensor_tensor(act_lo[:, 2 * pair:2 * pair + 2, :], scaled[pair % 2],
                                      act_hi[:, 2 * pair:2 * pair + 2, :].bitcast(F32),
                                      ALU.subtract).then_inc(act_ready, 1)
                    if pair + 2 < pairs:
                        dve.wait_ge(act_ready, pair + 1 + which * 2 * pairs)
                        scale_pair(pair + 2)
                    subtract_blocks("GM", n, between.get(pair, ()))

            def copy_params(first, last):
                dve.wait_ge(turned, last)
                for g in range(first, last):
                    row = sum(r for group in groups[:g] for _, r in group)
                    rows = sum(r for _, r in groups[g])
                    dve.tensor_copy(prm[:, row:row + rows], psum[:, SMALL_BANK, g * P:g * P + rows])\
                        .then_inc(prm_ready, 1)

            copy_params(0, 1)
            dve.wait_ge(cond_hi_ready, 1)
            parts = cond_w[:].rearrange("p k a -> p a k")
            dve.tensor_tensor(parts[:, 2:4, :], cond[:], parts[:, 0:2, :].bitcast(F32), ALU.subtract)\
                .then_inc(cond_ready, 1)
            subtract_blocks("M", 0, range(8))
            copy_params(1, len(groups))
            dve.wait_ge(exp_lam_ready, 1)
            dve.wait_ge(prm_ready, len(groups))
            lam = prm[:, column["lam"]:column["lam"] + 2 * HEADS]
            e, s, q, series, softplus = (small[:, j, :] for j in range(1, 6))
            then(dve.tensor_scalar(s, e, 2.0, None, ALU.add))
            then(dve.reciprocal(s, s))
            then(dve.tensor_tensor(s, s, e, ALU.mult))
            then(dve.tensor_tensor(q, s, s, ALU.mult))
            then(dve.tensor_scalar(series, q, ATANH_TERMS[0], None, ALU.mult))
            for term in ATANH_TERMS[1:]:
                then(dve.scalar_tensor_tensor(series, series, term, q, ALU.add, ALU.mult))
            then(dve.scalar_tensor_tensor(series, series, 1.0, s, ALU.add, ALU.mult))
            then(dve.tensor_scalar(softplus, lam, -1.0, 0.0, ALU.mult, ALU.max))
            then(dve.scalar_tensor_tensor(softplus, series, 2.0, softplus, ALU.mult, ALU.add))
            for j, factor in enumerate((LRU_C, -LRU_C, -2.0 * LRU_C)):
                dve.tensor_scalar(decay[:, j, :], softplus, factor, None, ALU.mult).then_inc(decay_ready, 1)

            dve.wait_ge(tables_landed, 32)
            for m in range(1, 5):
                n = 8 * m
                subtract_blocks("M", n, range(0, 1))
                copy_row(m - 1, n)
                subtract_blocks("M", n, range(1, 6))
                dve.wait_ge(x_turned, m)
                dve.wait_ge(ctx_copied, m)
                for a in range(4):
                    k = 4 * m - 4 + a
                    if k < KT // 2:
                        embed = pos_row[:, k, :].rearrange("p (r w) -> p r w", w=1)
                    else:
                        embed = pos_col[:, k - KT // 2, :].rearrange("p (r w) -> p r w", r=1)
                    last = dve.tensor_tensor(xT[:, k, CTX:T].rearrange("p (r w) -> p r w", w=GRID_W),
                                             psum[:, a, CTX:T].rearrange("p (r w) -> p r w", w=GRID_W),
                                             embed.broadcast_to([P, GRID_ROWS, GRID_W]), ALU.add)
                last.then_inc(x_ready, 1)
                subtract_blocks("M", n, range(6, 8))
                add_bias(m - 1)
            dve.wait_ge(x_ready, 4)
            dve.wait_ge(zeroed, 3)
            subtract_blocks("M", 40, range(0, 1))
            copy_row(4, 40)
            subtract_blocks("M", 40, range(1, 8))
            add_bias(4)
            make_rstd(0)
            with dve.Fori(6, MOD_FIRST) as i:
                n = i * 8
                subtract_blocks("M", n, range(0, 1))
                copy_row(i - 1, n)
                subtract_blocks("M", n, range(1, 8))
                add_bias(i - 1)

            def convolve(tile, row, weights, taps, first, to, scalar_bias):
                w = [prm[:, column[weights] + k * HEADS + tile:column[weights] + k * HEADS + tile + 1]
                     for k in range(taps)]
                source = padded[:, row, :]
                total = conv_sum[:, row, 0:RUN]
                if scalar_bias is None:
                    then(dve.tensor_scalar(total, source[:, first:first + RUN], w[0], None, ALU.mult))
                else:
                    then(dve.tensor_scalar(total, source[:, first:first + RUN], w[0], scalar_bias,
                                           ALU.mult, ALU.add))
                for k in range(1, taps - 1):
                    then(dve.scalar_tensor_tensor(total, source[:, first + k:first + k + RUN], w[k], total,
                                                  ALU.mult, ALU.add))
                k = taps - 1
                for start, at, length in ((0, 0, CTX), (CTX, SMP_AT - PAD, SMP)):
                    last = dve.scalar_tensor_tensor(to[:, start:start + length],
                                                    source[:, first + k + at:first + k + at + length], w[k],
                                                    total[:, at:at + length], ALU.mult, ALU.add)
                return last

            def drain_pair(phase, pair, bank, n_done):
                dve.wait_ge(block_done, n_done)
                own_before = {"v": pair + 1, "b": V_DRAINED + pair + 1}.get(phase)
                if own_before:
                    dve.wait_ge(drained, own_before)
                tiles = slice(2 * pair, 2 * pair + 2)
                gates = slice(HEADS + 2 * pair, HEADS + 2 * pair + 2)
                if phase == "x":
                    for a in range(2):
                        tile = 2 * pair + a
                        dve.wait_ge(padded_ready, tile + 1)
                        bias = column["conv_b"] + tile
                        convolve(tile, a, "conv_w", CONV, 0, mix[:, tile, :], prm[:, bias:bias + 1])\
                            .then_inc(xc_ready, 1)
                elif phase == "c":
                    dve.tensor_copy(mix[:, gates, :], banks(bank)).then_inc(drained, 1)
                elif phase == "v":
                    for a in range(2):
                        tile = 2 * pair + a
                        gated = mix[:, HEADS + tile, :]
                        dve.tensor_tensor(padded[:, a, CTX_AT:CTX_AT + CTX], psum[:, bank + a, 0:CTX],
                                          gated[:, 0:CTX], ALU.mult)
                        then(dve.tensor_tensor(padded[:, a, SMP_AT:SMP_AT + SMP], psum[:, bank + a, CTX:T],
                                               gated[:, CTX:T], ALU.mult))
                        last = convolve(tile, a, "sc_w", SC, 1, gated, None)
                        if a == 0:
                            then(last)
                    last.then_inc(drained, 1)
                elif phase == "b":
                    dve.tensor_tensor(mix[:, gates, :], mix[:, gates, :], banks(bank), ALU.mult)\
                        .then_inc(drained, 1)
                else:
                    dve.wait_ge(gelu_ready, pair + 1)
                    dve.wait_ge(head_done, 2 * pair + 2)
                    dve.tensor_tensor(mix[:, tiles, :], mix[:, tiles, :], gelu_y, ALU.mult).then_inc(drained, 1)

            def powers(head):
                dve.wait_ge(decays_ready, head + 1)
                dve.wait_ge(xc_ready, head + 1)
                both = mix[:, head:head + 1, :].broadcast_to([P, 2, T])
                then(dve.tensor_scalar(gate_r, gate_r, 1.0, None, ALU.add))
                dve.scalar_tensor_tensor(decay_t, decay_t, 0.0, gate_r, ALU.max, ALU.mult).then_inc(power_ready, 1)
                then(dve.tensor_tensor(gate_i, gate_i, both, ALU.mult))

            def scans(head):
                dve.wait_ge(root_u_ready, head + 1)
                then(dve.tensor_tensor(gate_i, gate_i, decay_t, ALU.mult))
                for d in range(2):
                    a, u, h = decay_a[:, d, :], gate_i[:, d, :], gate_r[:, d, :]
                    s = column["state"] + d * HEADS + head
                    for start, end, initial in ((0, CTX, 0.0), (CTX, T, prm[:, s:s + 1])):
                        tokens = slice(start, end) if d == 0 else slice(end - 1, start - 1 if start else None, -1)
                        last = dve.tensor_tensor_scan(h[:, tokens], a[:, tokens], u[:, tokens], initial,
                                                      ALU.mult, ALU.add)
                then(last)
                for d, token in ((0, CTX - 1), (1, 0)):
                    s = d * HEADS + head
                    dve.tensor_copy(stateT[:, s:s + 1], gate_r[:, d, token:token + 1])
                dve.tensor_tensor(mix[:, head, :], gate_r[:, 0, :], gate_r[:, 1, :], ALU.add)\
                    .then_inc(head_done, 1)

            for step in range(IN_STEPS):
                n = N_IN + 16 * step
                phase, turn = PHASES[step // 2][0], step % 2
                before = PHASES[(step - 1) // 2][0]
                head = step - FIRST_LRU
                if step == 0:
                    copy_row(MOD_FIRST - 1, n)
                    subtract_blocks("GM", n, range(0, 1))
                    add_bias(MOD_FIRST - 1)
                    dve.wait_ge(mod_ready, MOD_FIRST)
                    make_gain(0, 1)
                    norm_tiles(0, 0, n, {0: range(1, 2), 1: range(2, 4), 3: range(4, 6), 5: range(6, 8)})
                else:
                    subtract_blocks("GM", n, range(0, 2))
                    if head >= 1:
                        scans(head - 1)
                    subtract_blocks("GM", n, range(2, 3))
                    copy_row(MOD_FIRST + step - 1, n)
                    subtract_blocks("GM", n, range(3, 4))
                    drain_pair(before, 2 * ((step - 1) % 2) + 1, 2, n - 1)
                subtract_blocks("GM", n, range(4 if step else 8, 12))
                if step:
                    add_bias(MOD_FIRST + step - 1)
                drain_pair(phase, 2 * turn, 0, n + 7)
                subtract_blocks("GM", n, range(12, 15))
                if head >= 0:
                    powers(head)
                subtract_blocks("GM", n, range(15, 16))

            def residual_pair(pair, bank, n_done):
                dve.wait_ge(block_done, n_done)
                for a in range(2):
                    k = pair * 2 + a
                    for seg, start, end in SEGMENTS:
                        last = dve.scalar_tensor_tensor(
                            xT[:, bass.ds(k, 1), start:end].rearrange("p a t -> p (a t)"),
                            psum[:, bank + a, start:end],
                            modT[:, bass.ds(k + 2 * KT, 1), seg],
                            xT[:, bass.ds(k, 1), start:end].rearrange("p a t -> p (a t)"), ALU.mult, ALU.add)
                    if a == 1:
                        last.then_inc(x1_ready, 1)
            def add_pair(pair):
                dve.wait_ge(squared, pair + 5)
                then(dve.tensor_tensor(sumsq[:], sumsq[:], squares[:, 0, :], ALU.add))
                dve.tensor_tensor(sumsq[:], sumsq[:], squares[:, 1, :], ALU.add).then_inc(summed, 1)
                dve.wait_ge(summed, pair + 1)

            def out_step(n, i, first):
                subtract_blocks("GM", n, range(0, 3))
                copy_row(None, n)
                if not first:
                    subtract_blocks("GM", n, range(3, 4))
                if first:
                    for j in range(KT // 2):
                        pair = (j + KT // 4) % (KT // 2)
                        dve.wait_ge(act_hi_ready, KT // 2 + j + 1)
                        dve.tensor_tensor(act_lo[:, 2 * pair:2 * pair + 2, :], mix[:, 2 * pair:2 * pair + 2, :],
                                          act_hi[:, 2 * pair:2 * pair + 2, :].bitcast(F32), ALU.subtract)\
                            .then_inc(act_ready, 1)
                        if j == 1:
                            subtract_blocks("GM", n, range(3, 4))
                        if j == 2:
                            scans(HEADS - 1)
                            dve.wait_ge(mod_ready, 3 * KT // 4)
                            then(dve.memset(sumsq[:], 0.0))
                        if j == 3:
                            drain_pair("y", 3, 2, n - 1)
                        if j in (3, 5):
                            subtract_blocks("GM", n, range(j + 1, j + 3))
                else:
                    residual_pair(i * 2 - 1, 2, n - 1)
                    subtract_blocks("GM", n, range(4, 8))
                    add_pair(i * 2 - 1)
                subtract_blocks("GM", n, range(8, 12))
                add_bias(i + (MOD_FIRST + IN_STEPS - 1))
                residual_pair(i * 2, 0, n + 7)
                subtract_blocks("GM", n, range(12, 15))
                add_pair(i * 2)
                subtract_blocks("GM", n, range(15, 16))

            out_step(N_OUT, 0, True)
            with dve.Fori(1, OUT_STEPS) as i:
                own.enter(i - 1, 2)
                out_step(i * 16 + N_OUT, i, False)
                own.leave(OUT_STEPS - 1)

            def up_pair(chunk, pair, bank, n_done):
                dve.wait_ge(block_done, n_done)
                dve.wait_ge(silu_done, chunk * 2 + (pair + 1))
                tiles = silu_g[:, 2 * pair:2 * pair + 2, :]
                dve.tensor_tensor(tiles, tiles, banks(bank), ALU.mult).then_inc(h_full, 1)

            def low_h(chunk, pair):
                dve.wait_ge(h_hi_ready, chunk * 2 + (pair + 1))
                tiles = slice(2 * pair, 2 * pair + 2)
                dve.tensor_tensor(h_lo[:, tiles, :], silu_g[:, tiles, :], h_hi[:, tiles, :].bitcast(F32),
                                  ALU.subtract).then_inc(h_ready, 1)

            def down_pair(j, n_done, down_banks=DOWN_BANKS):
                dve.wait_ge(block_done, n_done)
                for a in range(2):
                    k = 2 * j + a
                    for seg, start, end in SEGMENTS:
                        last = dve.scalar_tensor_tensor(
                            xT[:, k, start:end], psum[:, down_banks[j] + a, start:end],
                            modT[:, 5 * KT + k, seg:seg + 1], xT[:, k, start:end], ALU.mult, ALU.add)
                last.then_inc(down_drained, 1)

            subtract_blocks("GM", N_G0, range(0, 2))
            residual_pair(KT // 2 - 1, 2, N_G0 - 1)
            copy_row(None, N_G0)
            add_pair(KT // 2 - 1)
            add_bias(MOD_STEPS - 3)
            dve.wait_ge(mod_ready, MOD_STEPS - 2)
            dve.wait_ge(x1_ready, KT // 2)
            make_gain(1, 4)
            subtract_blocks("GM", N_G0, range(2, 3))
            make_rstd(1)
            norm_tiles(1, 3, N_G0, {1: range(3, 4), 3: range(4, 6), 5: range(6, 8)})
            subtract_blocks("GM", N_G0, range(8, 16))
            subtract_blocks("GM", N_U0, range(0, 3))
            copy_row(None, N_U0)
            subtract_blocks("GM", N_U0, range(3, 4))
            subtract_blocks("GM", N_U0, range(4, 12))
            add_bias(MOD_STEPS - 2)
            up_pair(0, 0, UP_BANKS[0], N_U0 + 7)
            subtract_blocks("GM", N_U0, range(12, 14))
            low_h(0, 0)
            subtract_blocks("GM", N_U0, range(14, 16))
            subtract_blocks("G", N_G1, range(0, 4))
            copy_row(None, N_G1)
            up_pair(0, 1, FIRST_UP_BANKS[1], N_G1 - 1)
            subtract_blocks("G", N_G1, range(4, 5))
            low_h(0, 1)
            subtract_blocks("G", N_G1, range(5, 8))
            add_bias(MOD_STEPS - 1)
            dve.wait_ge(mod_ready, MOD_STEPS)

            def down_up_steps(n, chunk):
                subtract_blocks("D", n, range(0, 4))
                for j in range(4):
                    subtract_blocks("D", n, range(4 + j, 5 + j))
                    down_pair(j, n + j + 1)
                for j in range(4):
                    subtract_blocks("G", n + 8, range(j, j + 1))
                    down_pair(4 + j, n + j + 5)
                dve.wait_ge(down_drained, chunk * 8 + 8)
                subtract_blocks("G", n + 8, range(4, 8))
                up_pair(chunk + 1, 0, UP_BANKS[0], n + 8 + 4)

            with dve.Fori(0, TURNS) as i:
                n = i * PER_CHUNK + N_LOOP
                down_up_steps(n, i)
                subtract_blocks("G", n + 16, range(0, 1))
                low_h(i + 1, 0)
                subtract_blocks("G", n + 16, range(1, 4))
                up_pair(i + 1, 1, UP_BANKS[1], n + 16)
                subtract_blocks("G", n + 16, range(4, 5))
                low_h(i + 1, 1)
                subtract_blocks("G", n + 16, range(5, 8))
            down_up_steps(N_D, CHUNKS - 2)
            subtract_blocks("D", N_D + 16, range(0, 1))
            low_h(CHUNKS - 1, 0)
            subtract_blocks("D", N_D + 16, range(1, 3))
            up_pair(CHUNKS - 1, 1, UP_BANKS[1], N_D + 16)
            low_h(CHUNKS - 1, 1)
            subtract_blocks("D", N_D + 16, range(3, 4))
            then(dve.memset(sumsq[:], 0.0))

            def add_last_squares(pair):
                count = KT // 2 + pair + 1
                dve.wait_ge(squared, count + 4)
                then(dve.tensor_tensor(sumsq[:], sumsq[:], last_squares[pair % 2][:, 0, :], ALU.add))
                dve.tensor_tensor(sumsq[:], sumsq[:], last_squares[pair % 2][:, 1, :], ALU.add).then_inc(summed, 1)
                dve.wait_ge(summed, count)

            for j in range(8):
                if j < 4:
                    subtract_blocks("D", N_D + 16, range(4 + j, 5 + j))
                down_pair(j, N_D + 16 + j + 1, LAST_DOWN_BANKS)
                if j:
                    add_last_squares(j - 1)
            add_last_squares(7)
            dve.wait_ge(root_ready, 3)
            dve.reciprocal(token_rstd[:], token_rstd[:]).then_inc(rstd_ready, 1)
            dve.wait_ge(rstd_ready, 3)
            dve.wait_ge(y_copied, KT // 4)
            for half in range(2):
                if half:
                    dve.wait_ge(y_copied, KT // 2)
                for a in range(2):
                    cols = slice(D // 2 * half, D // 2 * (half + 1))
                    dve.tensor_scalar(x_rows[:, a, cols], x_rows[:, a, cols], token_rstd[:, a:a + 1], None,
                                      ALU.mult).then_inc(y_done, 1)

        @block_ctx.tensor
        def _(pe):
            def product(bank, hi, lo, x_hi, x_lo, first, last):
                pe.matmul(psum[:, bank, 0:T], hi, x_hi, start=first, stop=False)
                pe.matmul(psum[:, bank, 0:T], hi, x_lo, start=False, stop=False)
                return pe.matmul(psum[:, bank, 0:T], lo, x_hi, start=False, stop=last)

            def gemm_block(n, kind, b, bank, x_hi, x_lo, k0, first, last, acts=None, sem=act_ready):
                pe.wait_ge(lo_ready, n + 1)
                hi, lo = split_view(w_hi, kind, b), split_view(w_lo, kind, b)
                for kk in range(4):
                    if acts is not None and kk % 2 == 0:
                        pe.wait_ge(sem, acts + kk // 2)
                    for o in range(2):
                        out = product(bank + o, hi[:, kk, o * P:(o + 1) * P], lo[:, kk, o * P:(o + 1) * P],
                                      x_hi[:, k0 + kk, :], x_lo[:, k0 + kk, :],
                                      first and kk == 0, last and kk == 3)
                out.then_inc(block_done, 1)

            def mod_block(n, kind, b, k0):
                pe.wait_ge(lo_ready, n + 1)
                hi, lo = split_view(w_hi, kind, b), split_view(w_lo, kind, b)
                for kk in range(2):
                    k = k0 + kk
                    pe.matmul(psum[0:4, MOD_BANK, :], cond_w[:, k, :], hi[:, kk, :], start=k == 0, stop=False)
                    out = pe.matmul(psum[0:4, MOD_BANK, :], cond_w[:, k, :], lo[:, kk, :], start=False,
                                    stop=k == KT - 1)
                out.then_inc(block_done, 1)

            def turn_row(m):
                pe.wait_ge(row_ready, m + 1)
                if not isinstance(m, int) or m:
                    pe.wait_ge(mod_ready, m)
                for a in range(4):
                    out = pe.matmul(psum[:, SMALL_BANK, 2 * a:2 * a + 2], mod_row[:, a * P:(a + 1) * P], select[:],
                                    start=True, stop=True)
                out.then_inc(row_turned, 1)

            def gm_step(n, m, bank_free, acts=None, k_order=(0, 1), turn_at=5, gates=None, pair_banks=(0, 2)):
                for b in range(16):
                    pair, j = b // 8, (b % 8) // 2
                    if b == turn_at:
                        turn_row(m - 1)
                    if gates is not None and b % 8 == 0:
                        gates(pair)
                    if b % 2 == 0:
                        if j == 0:
                            bank_free(pair)
                        gemm_block(n + b, "GM", b, pair_banks[pair], act_hi, act_lo,
                                   8 * k_order[j // 2] + 4 * (j % 2), j == 0, j == 3,
                                   acts + 2 * j + 1 if acts is not None and pair == 0 else None)
                    else:
                        if b == 1:
                            pe.wait_ge(row_ready, m)
                        mod_block(n + b, "GM", b, 2 * (b // 2))

            def turn_params(first, last):
                for g in range(first, last):
                    rows = sum(r for _, r in groups[g])
                    pe.transpose(psum[:, SMALL_BANK, g * P:g * P + rows], prm_rows[0:rows, g, :],
                                 ident[0:rows, 0:rows]).then_inc(turned, 1)

            def mod_step(m, blocks=range(8)):
                if blocks[0] == 0 and (not isinstance(m, int) or m):
                    pe.wait_ge(row_ready, m)
                for b in blocks:
                    mod_block(m * 8 + b, "M", b, 2 * b)
                    if b == 4 and (not isinstance(m, int) or m):
                        turn_row(m - 1)

            pe.wait_ge(cond_landed, 48)
            turn_params(0, 1)
            pe.wait_ge(cond_ready, 1)
            mod_step(0)
            pe.wait_ge(params_landed, 16 * (len(sizes) - 2))
            turn_params(1, len(groups))
            pe.wait_ge(tables_landed, 32)
            pe.wait_ge(x_landed, 48)
            pe.wait_ge(prm_ready, len(groups))
            pe.wait_ge(zeroed, 2)

            def sum_squares(four):
                pe.wait_ge(squared, four)
                for a in range(4):
                    out = pe.matmul(psum[:, SUM_BANK, 0:T], ones[:], x_squares[:, a, :],
                                    start=four == 1 and a == 0, stop=four == 4 and a == 3)
                out.then_inc(sum_done, 1)

            for m in range(1, 5):
                mod_step(m, range(0, 2))
                if m >= 2:
                    pe.wait_ge(x_ready, m - 1)
                for k in range(4):
                    for a in range(3):
                        at = (4 * m - 4 + k) * P
                        out = pe.transpose(psum[:, k, a * P:(a + 1) * P], x_rows[:, a, at:at + P], ident[:])
                out.then_inc(x_turned, 1)
                if m >= 2:
                    sum_squares(m - 1)
                mod_step(m, range(2, 8))
            mod_step(5, range(0, 2))
            sum_squares(4)
            mod_step(5, range(2, 8))
            with pe.Fori(6, MOD_FIRST) as i:
                mod_step(i)

            def head_gates(head, direction):
                if direction == 0:
                    pe.wait_ge(gate_w_landed, head * 32 + 32)
                    pe.wait_ge(xc_ready, head + 1)
                if direction or not isinstance(head, int) or head:
                    pe.wait_ge(gates_read, head * 2 + direction)
                for bank, which in ((R_BANK, direction), (I_BANK, 2 + direction)):
                    out = pe.matmul(psum[:, bank, 0:T], gate_w[:, which, :],
                                    mix[:, bass.ds(head, 1), :].rearrange("p a t -> p (a t)"), start=True, stop=True)
                out.then_inc(gates_done, 1)

            pairs = KT // 2
            pe.wait_ge(root_ready, 1)
            gm_step(N_IN, MOD_FIRST, lambda pair: None, acts=0, turn_at=0)
            gm_step(N_IN + 16, MOD_FIRST + 1, lambda pair: pe.wait_ge(padded_ready, 2 * pair + 2))
            gm_step(N_IN + 32, MOD_FIRST + 2, lambda pair: pe.wait_ge(padded_ready, 2 * pair + 6),
                    gates=lambda direction: head_gates(0, direction))
            with pe.Fori(3, IN_STEPS) as i:
                gm_step(i * 16 + N_IN, i + MOD_FIRST, lambda pair: pe.wait_ge(drained, i * 2 + (pair - 5)),
                        gates=lambda direction: head_gates(i - FIRST_LRU, direction))
            gm_step(N_OUT, MOD_FIRST + IN_STEPS, lambda pair: pe.wait_ge(drained, 2 * IN_STEPS + pair - 5),
                    acts=pairs, k_order=(1, 0))
            with pe.Fori(1, OUT_STEPS) as i:
                gm_step(i * 16 + N_OUT, i + (MOD_FIRST + IN_STEPS), lambda pair: pe.wait_ge(x1_ready, i * 2 + (pair - 1)),
                        k_order=(1, 0))

            def g_step(n, pair_banks, bank_free, turn=False):
                for b in range(8):
                    if b % 4 == 0:
                        bank_free(b // 4)
                    gemm_block(n + b, "G", b, pair_banks[b // 4], act_hi, act_lo, 4 * (b % 4), b % 4 == 0, b % 4 == 3)
                    if turn and b == 3:
                        turn_row(MOD_STEPS - 1)

            def d_step(n, chunk):
                pe.wait_ge(h_ready, chunk * 2 + 2)
                for b in range(8):
                    if b in (2, 3):
                        pe.wait_ge(silu_done, chunk * 2 + (b + 1))
                    if b >= 4:
                        pe.wait_ge(down_drained, chunk * 8 + (b - 3))
                    gemm_block(n + b, "D", b, DOWN_BANKS[b], h_hi, h_lo, 0, True, True)

            def turn_pair(pair):
                pe.wait_ge(y_ready, pair + 1)
                if pair:
                    pe.wait_ge(y_copied, pair)
                for k in range(2):
                    for a in range(3):
                        at = 256 * (pair % 2) + k * P
                        out = pe.transpose(psum[:, a, at:at + P], y_tiles[pair % 2][:, k, a * P:(a + 1) * P], ident[:])
                out.then_inc(y_turned, 1)

            turn_row(MOD_STEPS - 3)
            pe.wait_ge(summed, KT // 2)
            pe.matmul(psum[:, SUM_BANK, 0:T], ones[:], sumsq[:], start=True, stop=True).then_inc(sum_done, 1)
            pe.wait_ge(root_ready, 2)
            gm_step(N_G0, MOD_STEPS - 2, lambda pair: pe.wait_ge(x1_ready, 2 * OUT_STEPS - 1 + pair),
                    acts=2 * pairs, turn_at=None)
            gm_step(N_U0, MOD_STEPS - 1, lambda pair: pe.wait_ge(silu_done, 2) if pair else None,
                    pair_banks=FIRST_UP_BANKS)
            pe.wait_ge(silu_done, 1)
            g_step(N_G1, (0, 2), lambda pair: pe.wait_ge(h_full, 2) if pair else None, turn=True)
            pe.wait_ge(mod_ready, MOD_STEPS)
            with pe.Fori(0, TURNS) as i:
                n = i * PER_CHUNK + N_LOOP
                d_step(n, i)
                g_step(n + 8, UP_BANKS, lambda pair: pe.wait_ge(down_drained, i * 8 + (pair + 5)))
                g_step(n + 16, (0, 2), lambda pair: pe.wait_ge(down_drained, i * 8 + (pair + 7)))
            d_step(N_D, CHUNKS - 2)
            g_step(N_D + 8, UP_BANKS, lambda pair: pe.wait_ge(down_drained, 8 * (CHUNKS - 2) + pair + 5))

            last = CHUNKS - 1
            pe.wait_ge(h_full, last * 2 + 1)
            for b in range(8):
                if b >= 2:
                    pe.wait_ge(down_drained, last * 8 + (b - 1))
                gemm_block(N_D + 16 + b, "D", b, LAST_DOWN_BANKS[b], h_hi, h_lo, 0, True, True,
                           None if b else last * 2 + 1, h_ready)
                if b >= 2:
                    turn_pair(b - 2)
            turn_pair(6)
            pe.wait_ge(summed, 2 * (KT // 2))
            pe.wait_ge(down_drained, 8 * CHUNKS)
            for a in range(3):
                out = pe.matmul(psum[:, TOKEN_BANK, a:a + 1], sumsq[:, a * P:(a + 1) * P], ones[:, 0:1],
                                start=True, stop=True)
            out.then_inc(sum_done, 1)
            turn_pair(7)
            pe.transpose(psum[0:2 * HEADS, STATE_BANK, 0:P], stateT[:], ident[:]).then_inc(state_turned, 1)


INPUTS = ["x_prompt", "x_sample", "state_rglru", "c", "c_ctx", "w_mod", "b_mod", "norm_g", "w_in", "lru_conv_w",
          "lru_conv_b", "lru_w_a", "lru_b_a", "lru_w_i", "lru_b_i", "lru_lambda", "sc_conv_w", "w_out", "w_gate",
          "w_up", "w_down", "final_g"]


def shape_tables(d_model, tokens):
    n_freq = d_model // 4
    freqs = np.float32(1.0) / np.float32(POS_BASE) ** (np.arange(n_freq, dtype=np.float32) / np.float32(n_freq))
    parts = []
    for count in (tokens // GRID_W, GRID_W):
        angle = freqs[:, None] * np.arange(count, dtype=np.float32)
        both = np.concatenate([np.sin(angle), np.cos(angle)]).reshape(-1, P, count)
        parts.append(both.transpose(1, 0, 2).reshape(P, -1))
    pick = np.zeros((P, 2), np.float32)
    pick[np.arange(4), np.arange(4) % 2] = 1.0
    return np.ascontiguousarray(np.concatenate(parts + [np.eye(P), pick], 1), np.float32)


def kernel(**inputs):
    import concourse.bacc as bacc
    from concourse.bass_utils import run_bass_kernel_spmd

    nc = bacc.Bacc("TRN2", target_bir_lowering=False, num_devices=1)
    arrays = {name: np.ascontiguousarray(inputs[name]) for name in INPUTS}
    arrays["tables"] = shape_tables(arrays["x_sample"].shape[2], arrays["x_sample"].shape[1])
    args = [nc.dram_tensor(f"in_{name}", a.shape, mybir.dt.from_np(a.dtype), kind="ExternalInput").ap()
            for name, a in arrays.items()]
    batch, _, _, width = arrays["state_rglru"].shape
    outputs = {"y_prompt": arrays["x_prompt"].shape, "y_sample": arrays["x_sample"].shape,
               "new_state": (arrays["x_prompt"].shape[0], arrays["state_rglru"].shape[1], 2, width)}
    args += [nc.dram_tensor(name, shape, F32, kind="ExternalOutput").ap() for name, shape in outputs.items()]
    build(nc, *args)
    result = run_bass_kernel_spmd(nc, [{f"in_{name}": a for name, a in arrays.items()}], core_ids=[0])
    return tuple(result.results[0][name] for name in outputs)
```
